# Optimizing a Trainium2 kernel written in Bass

```python
import jax
import jax.numpy as jnp
from jax import lax
import numpy as np

D_MODEL = 2048
BATCH = 1
SEQ = 256
DEPTH = 1

MIX_WIDTH = D_MODEL
HGRN_WIDTH = MIX_WIDTH // 2
HGRN_HEAD_DIM = 128
HGRN_HEADS = HGRN_WIDTH // HGRN_HEAD_DIM
HGRN_CHUNK = 64
ATTN_WIDTH = MIX_WIDTH - HGRN_WIDTH
ATTN_HEAD_DIM = 64
ATTN_Q_HEADS = ATTN_WIDTH // ATTN_HEAD_DIM
ATTN_KV_HEADS = 4
ATTN_GROUP = ATTN_Q_HEADS // ATTN_KV_HEADS
WINDOW = 128
ATTN_BLOCK = 128
REL_BUCKETS = 32
REL_MAX_DIST = 128
D_FF = -(-8 * D_MODEL // (3 * 256)) * 256
KV_WIDTH = ATTN_KV_HEADS * ATTN_HEAD_DIM
IN_SPLITS = (HGRN_WIDTH, HGRN_WIDTH, HGRN_WIDTH, HGRN_WIDTH, ATTN_WIDTH, KV_WIDTH, KV_WIDTH)
IN_WIDTH = sum(IN_SPLITS)
EPS = 1e-6
NEG_INF = -1e30

kernel_name = "hymba_hgrn2_swa_sink_adaln"

def rms_norm(x, w):
    xf = x.astype(jnp.float32)
    y = xf * lax.rsqrt(jnp.mean(xf * xf, axis=-1, keepdims=True) + EPS)
    return (y * w.astype(jnp.float32)).astype(x.dtype)

def t5_causal_buckets(dist):
    max_exact = REL_BUCKETS // 2
    d = np.maximum(dist, 0)
    log_b = max_exact + (np.log(np.maximum(d, 1) / max_exact)
                         / np.log(REL_MAX_DIST / max_exact)
                         * (REL_BUCKETS - max_exact)).astype(np.int32)
    log_b = np.minimum(log_b, REL_BUCKETS - 1)
    return np.where(d < max_exact, d, log_b).astype(np.int32)

def hgrn2_chunkwise(q, f_logit, i_in, lb):
    B, S, _ = q.shape
    C, H, dk = HGRN_CHUNK, HGRN_HEADS, HGRN_HEAD_DIM
    N = S // C
    f = lb + (1.0 - lb) * jax.nn.sigmoid(f_logit.astype(jnp.float32))
    k = 1.0 - f
    log_f = jnp.log(f)

    def heads(t):
        return t.astype(jnp.float32).reshape(B, N, C, H, dk)

    qc, kc, vc, gc = heads(q), heads(k), heads(i_in), heads(log_f)
    b = jnp.cumsum(gc, axis=2)
    b_mid = b[:, :, C // 2 - 1:C // 2]
    q_rel = qc * jnp.exp(b - b_mid)
    k_rel = kc * jnp.exp(b_mid - b)
    causal = jnp.asarray(np.tril(np.ones((C, C), dtype=bool)))
    a = jnp.einsum('bnthd,bnshd->bnhts', q_rel, k_rel)
    a = jnp.where(causal, a, 0.0)
    o_intra = jnp.einsum('bnhts,bnshe->bnthe', a, vc)

    b_last = b[:, :, -1]
    k_dec = kc * jnp.exp(b_last[:, :, None] - b)
    kv = jnp.einsum('bnshd,bnshe->bnhde', k_dec, vc)
    decay = jnp.exp(b_last)

    def step(state, inp):
        dec, kv_n = inp
        return dec[..., None] * state + kv_n, state

    s0 = jnp.zeros((B, H, dk, dk), jnp.float32)
    _, s_prev = lax.scan(step, s0, (jnp.moveaxis(decay, 1, 0), jnp.moveaxis(kv, 1, 0)))
    s_prev = jnp.moveaxis(s_prev, 0, 1)
    o_inter = jnp.einsum('bnthd,bnhde->bnthe', qc * jnp.exp(b), s_prev)
    return (o_intra + o_inter).reshape(B, S, H, dk)

def sliding_window_gqa(q, k, v, sinks, rel_table):
    B, S, _ = q.shape
    L, Hkv, G, dh = ATTN_BLOCK, ATTN_KV_HEADS, ATTN_GROUP, ATTN_HEAD_DIM
    NB = S // L
    qb = q.reshape(B, NB, L, Hkv, G, dh)
    pad = ((0, 0), (L, 0), (0, 0))
    kp = jnp.pad(k, pad).reshape(B, NB + 1, L, Hkv, dh)
    vp = jnp.pad(v, pad).reshape(B, NB + 1, L, Hkv, dh)
    kb = jnp.concatenate([kp[:, :-1], kp[:, 1:]], axis=2)
    vb = jnp.concatenate([vp[:, :-1], vp[:, 1:]], axis=2)

    scores = jnp.einsum('bnqhgd,bnkhd->bnhgqk', qb, kb).astype(jnp.float32) * (dh ** -0.5)
    qi = np.arange(L)[:, None]
    kj = np.arange(2 * L)[None, :]
    dist = qi + L - kj
    in_window = (dist >= 0) & (dist < WINDOW)
    key_pos = np.arange(NB)[:, None] * L - L + np.arange(2 * L)[None, :]
    valid = in_window[None] & (key_pos >= 0)[:, None, :]
    bias = rel_table[t5_causal_buckets(dist)].astype(jnp.float32)
    bias = jnp.transpose(bias, (2, 0, 1)).reshape(Hkv, G, L, 2 * L)
    scores = jnp.where(jnp.asarray(valid)[None, :, None, None], scores + bias, NEG_INF)
    sink = sinks.astype(jnp.float32).reshape(Hkv, G)[None, None, :, :, None, None]
    sink = jnp.broadcast_to(sink, scores.shape[:-1] + (1,))
    probs = jax.nn.softmax(jnp.concatenate([scores, sink], axis=-1), axis=-1)[..., :-1]
    out = jnp.einsum('bnhgqk,bnkhd->bnqhgd', probs.astype(v.dtype), vb)
    return out.reshape(B, S, Hkv * G * dh)

def setup_inputs(seed: int = 0) -> dict:
    key = jax.random.key(seed)
    ks = jax.random.split(key, 16)

    def nrm(k, shape, scale):
        return jax.random.normal(k, shape, jnp.float32) * scale

    return {
        "x": nrm(ks[0], (BATCH, SEQ, D_MODEL), 1.0),
        "c": nrm(ks[1], (BATCH, D_MODEL), 1.0),
        "w_ada": nrm(ks[2], (DEPTH, D_MODEL, 6 * D_MODEL), 0.5 * D_MODEL ** -0.5),
        "b_ada": nrm(ks[3], (DEPTH, 6 * D_MODEL), 0.01),
        "norm1_w": 1.0 + nrm(ks[4], (DEPTH, D_MODEL), 0.02),
        "w_in": nrm(ks[5], (DEPTH, D_MODEL, IN_WIDTH), D_MODEL ** -0.5),
        "lower_bounds": nrm(ks[6], (DEPTH + 1, HGRN_WIDTH), 0.5),
        "hgrn_norm_w": 1.0 + nrm(ks[7], (DEPTH, HGRN_WIDTH), 0.02),
        "attn_sinks": nrm(ks[8], (DEPTH, ATTN_Q_HEADS), 1.0),
        "rel_bias_table": nrm(ks[9], (REL_BUCKETS, ATTN_Q_HEADS), 0.5),
        "w_out": nrm(ks[10], (DEPTH, MIX_WIDTH, D_MODEL), MIX_WIDTH ** -0.5),
        "norm2_w": 1.0 + nrm(ks[11], (DEPTH, D_MODEL), 0.02),
        "w_gate": nrm(ks[12], (DEPTH, D_MODEL, D_FF), D_MODEL ** -0.5),
        "w_up": nrm(ks[13], (DEPTH, D_MODEL, D_FF), D_MODEL ** -0.5),
        "w_down": nrm(ks[14], (DEPTH, D_FF, D_MODEL), D_FF ** -0.5),
        "final_norm_w": 1.0 + nrm(ks[15], (D_MODEL,), 0.02),
    }

def reference(x, c, w_ada, b_ada, norm1_w, w_in, lower_bounds, hgrn_norm_w, attn_sinks,
              rel_bias_table, w_out, norm2_w, w_gate, w_up, w_down, final_norm_w):
    B, S, _ = x.shape
    offsets = list(np.cumsum(IN_SPLITS)[:-1])
    lb_all = jnp.cumsum(jax.nn.softmax(lower_bounds.astype(jnp.float32), axis=0), axis=0)
    c_act = jax.nn.silu(c)
    for layer in range(DEPTH):
        mod = c_act @ w_ada[layer] + b_ada[layer]
        shift1, scale1, gate1, shift2, scale2, gate2 = jnp.split(mod[:, None, :], 6, axis=-1)

        h = rms_norm(x, norm1_w[layer]) * (1 + scale1) + shift1
        proj = h @ w_in[layer]
        hq, hf, hi, hg, aq, ak, av = jnp.split(proj, offsets, axis=-1)

        o_rec = hgrn2_chunkwise(hq, hf, hi, lb_all[layer])
        o_rec = o_rec * lax.rsqrt(jnp.mean(o_rec * o_rec, axis=-1, keepdims=True) + EPS)
        o_rec = o_rec.reshape(B, S, HGRN_WIDTH) * hgrn_norm_w[layer].astype(jnp.float32)
        o_rec = (o_rec * jax.nn.silu(hg.astype(jnp.float32))).astype(x.dtype)

        o_att = sliding_window_gqa(aq, ak, av, attn_sinks[layer], rel_bias_table)

        mixed = jnp.concatenate([o_rec, o_att], axis=-1)
        x = x + gate1 * (mixed @ w_out[layer])

        h = rms_norm(x, norm2_w[layer]) * (1 + scale2) + shift2
        ffn = (jax.nn.silu(h @ w_gate[layer]) * (h @ w_up[layer])) @ w_down[layer]
        x = x + gate2 * ffn
    return rms_norm(x, final_norm_w)


_drawn_inputs = setup_inputs


def setup_inputs(seed=0):
    import zlib

    import numpy as np

    out = dict(_drawn_inputs(seed))
    spreads = {}
    factors = {'b_ada': 5.091,
     'norm1_w': 8.0,
     'hgrn_norm_w': 8.0,
     'attn_sinks': 64.0,
     'rel_bias_table': 2.851,
     'norm2_w': 8.0,
     'final_norm_w': 7.484}
    for name, (base, spread) in spreads.items():
        noise = np.random.default_rng([zlib.crc32(name.encode()), seed]).standard_normal(out[name].shape)
        drawn = base * np.exp(spread * noise) if base else spread * noise
        out[name] = jnp.asarray(drawn.astype(out[name].dtype))
    for name, factor in factors.items():
        out[name] = (out[name] * factor).astype(out[name].dtype)
    return out
```

```python
from contextlib import ExitStack

import concourse.bass as bass
import concourse.mybir as mybir

ALU = mybir.AluOpType
ACT = mybir.ActivationFunctionType
AX = mybir.AxisListType
F32 = mybir.dt.float32
F32R = mybir.dt.float32r
I32 = mybir.dt.int32

P = 128
D = 2048
S = 256
M = S // P
KC = D // P
N = 512
TK = 2
RING = 4
LEAD = RING
HW = 1024
HH = HW // P
CH = 64
AH = 16
DH = 64
PAIRS = AH // 2
REL_BUCKETS, REL_MAX = 32, 128
F = 5632
FJ = F // N
FA = 6
FB = FJ - FA
EPS = 1e-6
NEG = -1e30

IN_COLS = [4096, 4608, 5120, 1024, 1536, 2048, 2560, 0, 512, 3072, 3584]
NJ = len(IN_COLS)
JOB_TILES = KC // TK
STRAIGHT = [(j, TK * i, i == 0, i == JOB_TILES - 1) for j in range(NJ) for i in range(JOB_TILES)]
IN_TILES = len(STRAIGHT)
HALF = JOB_TILES // 2
for n0 in (0,):
    for half in (1, 0):
        for n in (n0, n0 + 1):
            STRAIGHT += [(NJ + n, TK * (HALF * half + i), half == 1 and i == 0, half == 0 and i == HALF - 1)
                         for i in range(HALF)]
for n in (2, 3):
    STRAIGHT += [(NJ + n, TK * i, i == 0, i == JOB_TILES - 1) for i in range(JOB_TILES)]
NS = len(STRAIGHT)
JOB_END = {j: t for t, (j, _, _, last) in enumerate(STRAIGHT) if last}
OUT_JOBS = D // N
J_FFN = NJ + OUT_JOBS
T_GA = NS
T_DA = T_GA + 2 * JOB_TILES * FA
DT_A = FA * 4 // TK
T_GB = T_DA + OUT_JOBS * DT_A
T_DB = T_GB + 2 * JOB_TILES * FB
DT_B = FB * 4 // TK
T_END = T_DB + OUT_JOBS * DT_B
JOB_GA = J_FFN
JOB_DA = JOB_GA + 2 * FA
JOB_GB = JOB_DA + OUT_JOBS
JOB_DB = JOB_GB + 2 * FB

AC = 1024
ADA_0 = 4 * KC
ADA_G2_STRAIGHT = 8
ADA_STRAIGHT = 6 * KC + ADA_G2_STRAIGHT
SHIFT1, SCALE1, GATE1, SHIFT2, SCALE2, GATE2 = (KC * i for i in range(6))

Q_GAPS = (9, 17)
K_GAP = 25
ATT_GAP, ATT_PERIOD = 27, 5
HG_GAP, HG_PERIOD = 65, 3
FIN_GAPS = (92, 93, 94, 94)
G1_GAPS = (97, 97, 98, 98)
RED_GAP = {16: 4, 32: 5, 48: 6, 64: 7, 82: 8, 92: 9}


def build(nc, x, c, w_ada, b_ada, norm1_w, w_in, lower_bounds, hgrn_norm_w, attn_sinks,
          rel_bias_table, w_out, norm2_w, w_gate, w_up, w_down, final_norm_w, out):
    ctx = ExitStack()
    with ctx:
        base = (nc.sbuf_base + 31) // 32 * 32
        at = [base]

        def sb(name, shape, dt=F32, offset=None):
            size = 4
            for n in shape[1:]:
                size *= n
            if offset is None:
                offset = at[0]
                at[0] += (size + 31) // 32 * 32
            assert offset + size <= nc.sbuf_usable_end, (name, offset + size - nc.sbuf_usable_end)
            return nc.alloc_sbuf_tensor_at(name, shape, dt, offset=offset)

        def sem(name):
            return ctx.enter_context(nc.semaphore(name))

        x_sb = sb("x_sb", [P, M, D])
        h_hi = sb("h_hi", [P, KC, S], F32R)
        h_lo = sb("h_lo", [P, KC, S], F32R)
        w_raw = sb("w_raw", [P, RING, TK, N])
        w_hi = sb("w_hi", [P, RING, TK, N], F32R)
        w_lo = sb("w_lo", [P, RING, TK, N], F32R)
        ada = sb("ada", [P, RING, AC])
        acc = sb("acc", [P, 2, AC])
        ident = sb("ident", [P, P])
        upper = sb("upper", [P, 2, P])
        after = sb("after", [P, P])
        ones = sb("ones", [P, 1])
        flip = sb("flip", [P, P])
        c_act = sb("c_act", [P, KC])
        cols = sb("cols", [P, 2 * KC + HH])
        bada = sb("bada", [P, 6 * KC])
        mod = sb("mod", [P, 6 * KC])
        gain = sb("gain", [P, KC])
        sink = sb("sink", [P, AH])
        stat = sb("stat", [P, 64])
        decay = sb("decay", [P, 4])
        mix_hi_at = at[0]
        mixa_hi = sb("mixa_hi", [P, HH, S], F32R)
        mixa_lo = sb("mixa_lo", [P, HH, S], F32R)
        work = at[0]
        KB = 1024
        k_tok = sb("k_tok", [P, M, HW], offset=work)
        g_tok = sb("g_tok", [P, M, HW], offset=work + 8 * KB)
        v_tok = sb("v_tok", [P, M, HW], offset=work + 16 * KB)
        q_tok = sb("q_tok", [P, M, HW], offset=work + 24 * KB)
        k_dup = sb("k_dup", [P, M, 4, 2, DH], offset=work + 8 * KB)
        low = sb("low", [P, 2, HW], offset=work + 24 * KB)
        low_t = sb("low_t", [P, HW], offset=work + 16 * KB)
        qT = sb("qT", [P, PAIRS, S], offset=work + 32 * KB)
        silu_g = sb("silu_g", [P, M, HW], offset=work + 32 * KB)
        kT = sb("kT", [P, 4, S], offset=work + 40 * KB)
        v_att = sb("v_att", [P, M, 4 * DH], offset=work + 44 * KB)
        o_att = sb("o_att", [P, M, P], offset=work + 46 * KB)
        bias = sb("bias", [P, 4, 2 * P], offset=work + 47 * KB)
        probs = sb("probs", [P, 2, 3 * P], offset=work + 51 * KB)
        probsT = sb("probsT", [P, 2, 3 * P], offset=work + 54 * KB)
        gated = sb("gated", [P, M, N], offset=work + 51 * KB)
        hg = sb("hg", [P, 2, 4, S], offset=work + 57 * KB)
        modulated = sb("modulated", [P, 2, 2, S], offset=work + 57 * KB)
        state = sb("state", [P, 3, P], offset=work + 65 * KB)
        att = sb("att", [P, M, P], offset=work + 65 * KB + 1536)
        junk = sb("junk", [P, M, P], offset=work + 44 * KB)
        table_t = sb("table_t", [AH, REL_BUCKETS], offset=work + 32 * KB)
        bias_row = sb("bias_row", [AH, 3 * P], offset=work + 33 * KB)
        vec_rows = sb("vec_rows", [3 * KC + HH, P], offset=work + 16 * KB)
        bada_rows = sb("bada_rows", [6 * KC, P], offset=work + 17 * KB)
        xn = sb("xn", [P, M, D], offset=work)
        sq_junk = sb("sq_junk", [P, M, N], offset=work + 57 * KB)
        hid_hi = sb("hid_hi", [P, 4 * FA, S], F32R, offset=mix_hi_at)
        hid_lo = sb("hid_lo", [P, 4 * FA, S], F32R, offset=mix_hi_at + 24 * KB)
        hid_g = sb("hid_g", [P, M, N], offset=work + 32 * KB)
        hid_t = sb("hid_t", [P, M, N], offset=work + 36 * KB)
        gate_row = sb("gate_row", [P, D], offset=work + 40 * KB)
        gate1_row = sb("gate1_row", [P, D], offset=work + 8 * KB)
        final_row = sb("final_row", [P, D], offset=work + 32 * KB)
        y_sb = sb("y_sb", [P, M, D], offset=work)

        acc_ps = ctx.enter_context(nc.psum_tensor("acc_ps", [P, 4, N], F32))
        small_ps = ctx.enter_context(nc.psum_tensor("small_ps", [P, N], F32))
        misc_ps = ctx.enter_context(nc.psum_tensor("misc_ps", [P, 3, N], F32))

        bias_dram = nc.dram_tensor("bias_dram", (AH, 3 * P), F32, kind="Internal").ap()

        x_loaded = [sem(f"x_loaded{m}") for m in range(M)]
        vec_loaded = sem("vec_loaded")
        sink_loaded = sem("sink_loaded")
        low_loaded = sem("low_loaded")
        table_loaded = sem("table_loaded")
        bias_stored = sem("bias_stored")
        bias_loaded = [sem(f"bias_loaded{i}") for i in range(4)]
        final_loaded = sem("final_loaded")
        weight_loaded = [sem(f"weight_loaded{i}") for i in range(RING)]
        ada_loaded = [sem(f"ada_loaded{i}") for i in range(RING)]
        out_stored = sem("out_stored")

        consts_ready = sem("consts_ready")
        pool_chain = sem("pool_chain")
        act_chain = sem("act_chain")
        dve_chain = sem("dve_chain")

        hi_ready = sem("hi_ready")
        lo_ready = sem("lo_ready")
        tile_done = sem("tile_done")
        pair_free = [sem(f"pair_free{i}") for i in range(2)]

        vec_turned = sem("vec_turned")
        c_ready = sem("c_ready")
        ada_on_pe = sem("ada_on_pe")
        ada_on_dve = sem("ada_on_dve")
        block_summed = sem("block_summed")
        block_reduced = sem("block_reduced")
        mod_ready = sem("mod_ready")

        squares_ready = sem("squares_ready")
        root_ready = sem("root_ready")
        mean_ready = sem("mean_ready")
        xn_ready = sem("xn_ready")
        xn_turned = sem("xn_turned")
        modulated_ready = sem("modulated_ready")
        h_hi_ready = sem("h_hi_ready")
        h_lo_ready = sem("h_lo_ready")

        qk_turned = sem("qk_turned")
        qk_ready = sem("qk_ready")
        low_step = sem("low_step")
        sigmoid_ready = sem("sigmoid_ready")
        f_ready = sem("f_ready")
        logf_ready = sem("logf_ready")

        scores_ready = sem("scores_ready")
        max_ready = sem("max_ready")
        exp_ready = sem("exp_ready")
        den_ready = sem("den_ready")
        probs_turned = sem("probs_turned")
        probsT_ready = sem("probsT_ready")
        pv_ready = sem("pv_ready")
        o_att_ready = sem("o_att_ready")
        o_att_turned = sem("o_att_turned")
        mixa_hi_ready = sem("mixa_hi_ready")
        mixa_lo_ready = sem("mixa_lo_ready")

        sums_ready = sem("sums_ready")
        hg_exp_ready = sem("hg_exp_ready")
        hg_ops_ready = sem("hg_ops_ready")
        hg_scores_ready = sem("hg_scores_ready")
        hg_state_ready = sem("hg_state_ready")
        hg_out_ready = sem("hg_out_ready")
        hg_out_taken = sem("hg_out_taken")
        hg_normed = sem("hg_normed")
        hg_turned = sem("hg_turned")
        mixr_tmp_ready = sem("mixr_tmp_ready")
        mixr_hi_ready = sem("mixr_hi_ready")
        mixr_lo_ready = sem("mixr_lo_ready")

        gate_spread = sem("gate_spread")
        gate_row_ready = sem("gate_row_ready")
        gated_ready = sem("gated_ready")
        x_updated = sem("x_updated")
        hid_g_ready = sem("hid_g_ready")
        hid_t_ready = sem("hid_t_ready")
        hid_turned = sem("hid_turned")
        hid_hi_ready = sem("hid_hi_ready")
        hid_lo_ready = sem("hid_lo_ready")
        y_ready = sem("y_ready")

        x_dram = x.rearrange("b (m p) d -> p (b m) d", p=P)
        out_dram = out.rearrange("b (m p) d -> p (b m) d", p=P)
        wada = w_ada[0]

        def chunked(w, k0, nk, c0, n):
            return w[k0 * P:(k0 + nk) * P, bass.ds(c0, n)].rearrange("(c p) n -> p c n", p=P)

        def pair_of(job):
            return job % 2

        def job_free_count(job):
            return 2 * (job // 2)

        block = ctx.enter_context(nc.Block())

        @block.sync
        def _(sp):
            def load_weight(t, slot, src, first=False):
                if not first:
                    sp.wait_ge(lo_ready, t - (RING - 1))
                sp.dma_start(w_raw[:, slot], src).then_inc(weight_loaded[slot], 16)

            def load_ada(slot, src):
                sp.dma_start(ada[:, slot], src).then_inc(ada_loaded[slot], 16)

            for m in range(M):
                sp.dma_start(x_sb[:, m], x_dram[:, m]).then_inc(x_loaded[m], 16)
            for i in range(RING):
                load_ada(i, wada[i * P:(i + 1) * P, 0:AC])
            for kc in range(RING, 2 * KC):
                blk, k = divmod(kc, KC)
                if kc % 2 == 0:
                    sp.wait_ge(ada_on_pe, (kc - RING) // 2 + 1)
                else:
                    sp.wait_ge(ada_on_dve, (kc - RING) // 2 + 1)
                load_ada(kc % RING, wada[k * P:(k + 1) * P, blk * AC:(blk + 1) * AC])
            with sp.Fori(1, 2 + 1) as i:
                for kc in range(KC):
                    if kc % 2 == 0:
                        sp.wait_ge(ada_on_pe, i * (KC // 2) + (KC // 2 + (kc - RING) // 2 + 1))
                    else:
                        sp.wait_ge(ada_on_dve, i * (KC // 2) + (KC // 2 + (kc - RING) // 2 + 1))
                    load_ada(kc % RING, wada[kc * P:(kc + 1) * P, bass.ds(i * AC + AC, AC)])
            for t, (job, kc, _, _) in enumerate(STRAIGHT):
                if job < NJ:
                    src = chunked(w_in[0], kc, TK, IN_COLS[job], N)
                else:
                    src = chunked(w_out[0], kc, TK, (job - NJ) * N, N)
                load_weight(t, t % RING, src, first=t < RING)
                if t < ADA_STRAIGHT:
                    a = ADA_0 + t
                    if a - RING < ADA_0:
                        if a % 2 == 0:
                            sp.wait_ge(ada_on_pe, (a - RING) // 2 + 1)
                        else:
                            sp.wait_ge(ada_on_dve, (a - RING) // 2 + 1)
                    else:
                        sp.wait_ge(ada_on_dve, ADA_0 // 2 + (a - RING - ADA_0) + 1)
                    if t < 6 * KC:
                        blk, k = 4 + t // KC, t % KC
                    else:
                        k, blk = (t - 6 * KC) // 2, 10 + t % 2
                    load_ada(a % RING, wada[k * P:(k + 1) * P, blk * AC:(blk + 1) * AC])
            a_done = ADA_0 // 2 + ADA_STRAIGHT
            with sp.Fori(0, FA) as i:
                for u in range(2 * JOB_TILES):
                    w = w_gate[0] if u < JOB_TILES else w_up[0]
                    load_weight(i * (2 * JOB_TILES) + (T_GA + u), u % RING,
                                chunked(w, TK * (u % JOB_TILES), TK, i * N, N))
                    if u % 4 == 3:
                        v = u // 4
                        sp.wait_ge(ada_on_dve, i * 4 + (a_done + v - RING + 1))
                        k0 = (ADA_G2_STRAIGHT // 2 + v // 2) * P
                        load_ada(v, wada[bass.ds(i * (2 * P) + k0, P),
                                         (10 + v % 2) * AC:(11 + v % 2) * AC])

            def down(t0, f0, tiles, steps):
                with sp.Fori(0, steps) as i:
                    for u in range(2 * tiles):
                        jj, v = divmod(u, tiles)
                        load_weight(i * (2 * tiles) + (t0 + u), u % RING,
                                    chunked(w_down[0], f0 + TK * v, TK, i * (2 * N) + jj * N, N))

            down(T_DA, 0, DT_A, OUT_JOBS // 2)
            with sp.Fori(0, FB) as i:
                for u in range(2 * JOB_TILES):
                    w = w_gate[0] if u < JOB_TILES else w_up[0]
                    load_weight(i * (2 * JOB_TILES) + (T_GB + u), u % RING,
                                chunked(w, TK * (u % JOB_TILES), TK, i * N + FA * N, N))
            down(T_DB, 4 * FA, DT_B, OUT_JOBS // 2)
            sp.wait_ge(hid_lo_ready, 2 * FJ)
            sp.dma_start(final_row[:], final_norm_w.partition_broadcast(P)).then_inc(final_loaded, 16)
            for q in range(4):
                m, half = divmod(q, 2)
                sp.wait_ge(y_ready, q + 1)
                sp.dma_start(out_dram[:, m, half * AC:(half + 1) * AC],
                             y_sb[:, m, half * AC:(half + 1) * AC]).then_inc(out_stored, 16)
            sp.wait_ge(out_stored, 64)

        @block.tensor
        def _(pe):
            def transpose(dst, src, n=P):
                return pe.transpose(dst, src, ident[0:n, 0:n])

            def products(t, slot, pair, lhs, first, last):
                pe.wait_ge(lo_ready, t + 1)
                for kk in range(TK):
                    for m in range(M):
                        hi, lo = lhs(kk, m)
                        dst = acc_ps[:, 2 * pair + m]
                        pe.matmul(dst, hi, w_hi[:, slot, kk], start=first and kk == 0, stop=False)
                        pe.matmul(dst, hi, w_lo[:, slot, kk], start=False, stop=False)
                        mm = pe.matmul(dst, lo, w_hi[:, slot, kk], start=False,
                                       stop=last and kk == TK - 1)
                mm.then_inc(tile_done, 1)

            def of_h(kc):
                return lambda kk, m: (h_hi[:, kc + kk, m * P:(m + 1) * P],
                                      h_lo[:, kc + kk, m * P:(m + 1) * P])

            def of_mixed(kc):
                if kc >= HH:
                    return lambda kk, m: (mixa_hi[:, kc - HH + kk, m * P:(m + 1) * P],
                                          mixa_lo[:, kc - HH + kk, m * P:(m + 1) * P])
                return of_h(kc)

            def of_hidden(kc):
                return lambda kk, m: (hid_hi[:, kc + kk, m * P:(m + 1) * P],
                                      hid_lo[:, kc + kk, m * P:(m + 1) * P])

            def reduce_block(q, buf, col):
                pe.wait_ge(block_summed, q + 1)
                for cc in range(8):
                    mm = pe.matmul(small_ps[:, bass.ds(col + cc, 1)], acc[:, buf, cc * P:(cc + 1) * P],
                                   ones[:], start=False, stop=False, skip_group_check=True)
                mm.then_inc(block_reduced, 1)

            def turn_x(norm):
                for kp in range(KC // 2):
                    if kp == 0:
                        pe.wait_ge(xn_ready, 2 * norm + 2)
                    if kp >= 2:
                        pe.wait_ge(modulated_ready, 8 * norm + kp - 1)
                    for j in range(2):
                        for m in range(M):
                            kc = 2 * kp + j
                            tr = transpose(misc_ps[:, kp % 2, j * S + m * P:j * S + (m + 1) * P],
                                           xn[:, m, kc * P:(kc + 1) * P])
                    tr.then_inc(xn_turned, 1)

            pe.wait_ge(consts_ready, 1)
            pe.wait_ge(vec_loaded, 16 * 5)
            transpose(misc_ps[:, 2, 0:3 * KC + HH], vec_rows[:], 3 * KC + HH)
            transpose(misc_ps[:, 2, P:P + 6 * KC], bada_rows[:], 6 * KC).then_inc(vec_turned, 1)
            pe.wait_ge(c_ready, 1)
            pe.matmul(small_ps[:, N - 1:N], ident[:], ones[:], start=True, stop=False,
                      skip_group_check=True)
            with pe.Fori(0, 2) as i:
                for b in range(2):
                    for kc in range(0, KC, 2):
                        pe.wait_ge(ada_loaded[kc % RING], i * (16 * 8) + 16 * (4 * b + kc // 4 + 1))
                        for cc in range(8):
                            mm = pe.matmul(small_ps[:, bass.ds(i * KC + (8 * b + cc), 1)],
                                           ada[:, kc % RING, cc * P:(cc + 1) * P],
                                           c_act[:, kc:kc + 1], start=False, stop=False,
                                           skip_group_check=True)
                        mm.then_inc(ada_on_pe, 1)
                    pe.wait_ge(block_summed, i * 2 + (b + 1))
                    for cc in range(8):
                        mm = pe.matmul(small_ps[:, bass.ds(i * KC + (8 * b + cc), 1)],
                                       acc[:, b, cc * P:(cc + 1) * P], ones[:],
                                       start=False, stop=False, skip_group_check=True)
                    mm.then_inc(block_reduced, 1)
            turn_x(0)

            def att_scores(p):
                pe.wait_ge(qk_ready, 3)
                if p:
                    pe.wait_ge(probsT_ready, p)
                for a in range(2):
                    r = slice(DH * a, DH * a + DH)
                    h = 2 * p + a
                    pe.wait_ge(bias_loaded[h % 4], 16 * (h // 4 + 1))
                    for q, dst in ((0, misc_ps[:, a, 0:P]), (1, misc_ps[:, a, P:3 * P])):
                        pe.matmul(dst, flip[:], bias[:, h % 4, (1 - q) * P:], start=True, stop=False)
                        mm = pe.matmul(dst, qT[r, p, q * P:(q + 1) * P], kT[r, p // 2, 0:(q + 1) * P],
                                       start=False, stop=True)
                mm.then_inc(scores_ready, 1)

            def att_turn(p):
                pe.wait_ge(exp_ready, p + 1)
                for a in range(2):
                    for j in range(3):
                        tr = transpose(misc_ps[:, a, j * P:(j + 1) * P], probs[:, a, j * P:(j + 1) * P])
                tr.then_inc(probs_turned, 1)

            def att_pv(p):
                pe.wait_ge(probsT_ready, p + 1)
                if p:
                    pe.wait_ge(mixa_lo_ready, p)
                else:
                    pe.wait_ge(c_ready, 1)
                v = slice(DH * (p // 2), DH * (p // 2) + DH)
                for a in range(2):
                    o0 = misc_ps[:, 2, a * DH:(a + 1) * DH]
                    o1 = misc_ps[:, 2, P + a * DH:P + (a + 1) * DH]
                    pe.matmul(o0, probsT[:, a, 0:P], v_att[:, 0, v], start=True, stop=True)
                    pe.matmul(o1, probsT[:, a, P:2 * P], v_att[:, 0, v], start=True, stop=False)
                    mm = pe.matmul(o1, probsT[:, a, 2 * P:3 * P], v_att[:, 1, v], start=False, stop=True)
                mm.then_inc(pv_ready, 1)

            def att_turn_out(p):
                pe.wait_ge(o_att_ready, p + 1)
                for m in range(M):
                    tr = transpose(misc_ps[:, 2, 2 * P + m * P:2 * P + (m + 1) * P], o_att[:, m])
                tr.then_inc(o_att_turned, 1)

            def hg_prepare(h):
                hc = slice(h * P, (h + 1) * P)
                if h == 0:
                    pe.wait_ge(logf_ready, 2)
                    pe.wait_ge(mod_ready, 5)
                    pe.wait_ge(probsT_ready, PAIRS)
                    pe.wait_ge(pair_free[pair_of(7)], job_free_count(7) + 2)
                else:
                    pe.wait_ge(hg_exp_ready, h)
                    pe.wait_ge(hg_ops_ready, h)
                    pe.wait_ge(hg_state_ready, h)
                if h == HH // 2:
                    pe.wait_ge(pair_free[pair_of(8)], job_free_count(8) + 2)
                if h == 6:
                    pe.wait_ge(mod_ready, 6)
                for m in range(M):
                    pe.matmul(misc_ps[:, 0, m * S:(m + 1) * S], g_tok[:, m, hc],
                              upper[:].rearrange("p a b -> p (a b)"), start=True, stop=True)
                for m in range(M):
                    transpose(misc_ps[:, 1, m * P:(m + 1) * P], q_tok[:, m, hc])
                    transpose(misc_ps[:, 1, S + m * P:S + (m + 1) * P], k_tok[:, m, hc])
                for m in range(M):
                    mm = pe.matmul(small_ps[:, m * P:(m + 1) * P], after[:], g_tok[:, m, hc],
                                   start=True, stop=True, skip_group_check=True)
                mm.then_inc(sums_ready, 1)

            def hg_core(h):
                hc = slice(h * P, (h + 1) * P)
                t = hg[:, h % 2]
                pe.wait_ge(hg_ops_ready, h + 1)
                if h:
                    pe.wait_ge(hg_out_taken, h)
                else:
                    pe.wait_ge(mixa_lo_ready, PAIRS)
                for m in range(M):
                    pe.matmul(misc_ps[:, 2, m * P:(m + 1) * P], t[:, 1, m * P:(m + 1) * P],
                              t[:, 0, m * P:(m + 1) * P], start=True, stop=True)
                for ch in range(3):
                    m, r = ch // 2, slice(CH * (ch % 2), CH * (ch % 2) + CH)
                    dst = (misc_ps[:, 2, S:S + P], misc_ps[:, 0, 0:P], misc_ps[:, 2, S + P:S + 2 * P])[ch]
                    mm = pe.matmul(dst, t[r, 3, m * P:(m + 1) * P], v_tok[r, m, hc],
                                   start=True, stop=True)
                mm.then_inc(hg_scores_ready, 1)

            def hg_out(h):
                hc = slice(h * P, (h + 1) * P)
                t = hg[:, h % 2]
                pe.wait_ge(hg_state_ready, h + 1)
                for m in range(M):
                    cs = slice(m * P, (m + 1) * P)
                    pe.matmul(misc_ps[:, 2, cs], att[:, m], v_tok[:, m, hc],
                              start=True, stop=False, skip_group_check=True)
                    for r in range(2):
                        ch = 2 * m + r
                        if ch:
                            mm = pe.matmul(misc_ps[CH * r:CH * r + CH, 2, cs],
                                           t[:, 2, ch * CH:(ch + 1) * CH], state[:, ch - 1],
                                           start=False, stop=True, skip_group_check=True)
                mm.then_inc(hg_out_ready, 1)

            def hg_turn(i):
                pe.wait_ge(hg_normed, 1)
                if i == 0:
                    pe.wait_ge(hg_out_taken, HH)
                if i == 3:
                    pe.wait_ge(mixr_tmp_ready, 1)
                for j in range(2):
                    for m in range(M):
                        h = 2 * i + j
                        tr = transpose(misc_ps[:, i % 3, j * S + m * P:j * S + (m + 1) * P],
                                       k_tok[:, m, h * P:(h + 1) * P])
                tr.then_inc(hg_turned, 1)

            def spread_gate(n, col, which):
                if n == 3:
                    pe.wait_ge(gate_row_ready, 4 * which + 1)
                for j in range(4):
                    mm = pe.matmul(misc_ps[:, n % 3, j * P:(j + 1) * P],
                                   mod[:, col + 4 * n + j:col + 4 * n + j + 1].to_broadcast([P, P]),
                                   ident[:], start=True, stop=True)
                mm.then_inc(gate_spread, 1)

            def gap(g):
                if g in Q_GAPS:
                    u = Q_GAPS.index(g)
                    pe.wait_ge(pair_free[u], 2)
                    if u == 0:
                        pe.wait_ge(modulated_ready, 8)
                    else:
                        pe.wait_ge(qk_ready, u)
                    for b in range(4):
                        for m in range(M):
                            tr = transpose(misc_ps[:, b // 2, (b % 2) * S + m * P:(b % 2) * S + (m + 1) * P],
                                           k_tok[:, m, N * u + b * P:N * u + (b + 1) * P])
                    tr.then_inc(qk_turned, 1)
                if g == K_GAP:
                    pe.wait_ge(pair_free[0], 4)
                    pe.wait_ge(qk_ready, 2)
                    for b in range(4):
                        for m in range(M):
                            tr = transpose(misc_ps[:, b // 2, (b % 2) * S + m * P:(b % 2) * S + (m + 1) * P],
                                           k_dup[:, m, b].rearrange("p a b -> p (a b)"))
                    tr.then_inc(qk_turned, 1)
                if g in RED_GAP:
                    q = RED_GAP[g]
                    pe.wait_ge(mod_ready, q - 3)
                    if q >= 8:
                        pe.wait_ge(hg_exp_ready, 6 if q == 8 else HH)
                    reduce_block(q, q % 2, 8 * q)
                p, s = divmod(g - ATT_GAP, ATT_PERIOD)
                if 0 <= p < PAIRS:
                    {0: att_scores, 2: att_turn, 3: att_pv, 4: att_turn_out}.get(s, lambda p: None)(p)
                h, s = divmod(g - HG_GAP, HG_PERIOD)
                if s == 0:
                    if 0 <= h - 1 < HH:
                        hg_out(h - 1)
                    if 0 <= h < HH:
                        hg_prepare(h)
                if s == 2 and 0 <= h < HH:
                    hg_core(h)
                for i in range(4):
                    if FIN_GAPS[i] == g:
                        hg_turn(i)
                    if G1_GAPS[i] == g:
                        if i == 0:
                            pe.wait_ge(mixr_tmp_ready, 4)
                        spread_gate(i, GATE1, 0)

            for t, (job, kc, first, last) in enumerate(STRAIGHT):
                if first and job >= 2:
                    pe.wait_ge(pair_free[pair_of(job)], job_free_count(job))
                if job == 0:
                    pe.wait_ge(h_lo_ready, kc // 2 + 1)
                if job >= NJ:
                    if kc >= HH:
                        pe.wait_ge(mixa_lo_ready, PAIRS)
                    else:
                        pe.wait_ge(mixr_lo_ready, kc // 2 + 1)
                products(t, t % RING, pair_of(job), of_h(kc) if job < NJ else of_mixed(kc), first, last)
                gap(t)

            turn_x(1)

            def turn_hidden(count):
                pe.wait_ge(hid_t_ready, count * 2 + 2)
                pe.wait_ge(hid_lo_ready, count * 2)
                for b in range(2):
                    for j in range(2):
                        for m in range(M):
                            tr = transpose(misc_ps[:, b, j * S + m * P:j * S + (m + 1) * P],
                                           hid_t[:, m, (2 * b + j) * P:(2 * b + j + 1) * P])
                    tr.then_inc(hid_turned, 1)

            def gate_up(i, t0, job0, before, peeled):
                for jj in range(2):
                    job = job0 + jj
                    pe.wait_ge(pair_free[pair_of(job)], i * 2 + job_free_count(job))
                    for v in range(JOB_TILES):
                        u = jj * JOB_TILES + v
                        if peeled and before == 0 and jj == 0:
                            pe.wait_ge(h_lo_ready, 8 + v + 1)
                        products(i * (2 * JOB_TILES) + (t0 + u), u % RING, pair_of(job), of_h(TK * v),
                                 v == 0, v == JOB_TILES - 1)
                        if not peeled and u == 2:
                            turn_hidden(i + (before - 1))

            def down(t0, job0, tiles, steps, last_hidden):
                with pe.Fori(0, steps) as i:
                    for jj in range(2):
                        job = job0 + jj
                        pe.wait_ge(pair_free[pair_of(job)], i * 2 + job_free_count(job))
                        for v in range(tiles):
                            if v == tiles - 2:
                                pe.wait_ge(hid_lo_ready, last_hidden)
                            u = jj * tiles + v
                            products(i * (2 * tiles) + (t0 + u), u % RING, pair_of(job),
                                     of_hidden(TK * v), v == 0, v == tiles - 1)

            gate_up(0, T_GA, JOB_GA, 0, True)
            with pe.Fori(1, FA) as i:
                gate_up(i, T_GA, JOB_GA, 0, False)
            pe.wait_ge(block_summed, 12)
            for q in (10, 11):
                reduce_block(q, q % 2, 8 * q)
            turn_hidden(FA - 1)
            pe.wait_ge(mod_ready, 8)
            pe.wait_ge(hid_lo_ready, 2 * FA)
            for n in range(4):
                spread_gate(n, GATE2, 1)
            down(T_DA, JOB_DA, DT_A, OUT_JOBS // 2, 2 * FA)
            gate_up(0, T_GB, JOB_GB, FA, True)
            with pe.Fori(1, FB) as i:
                gate_up(i, T_GB, JOB_GB, FA, False)
            turn_hidden(FJ - 1)
            down(T_DB, JOB_DB, DT_B, OUT_JOBS // 2, 2 * FJ)

        @block.scalar
        def _(act):
            chain = [0]

            def link(ins):
                chain[0] += 1
                ins.then_inc(act_chain, 1)
                act.wait_ge(act_chain, chain[0])

            def split(t, slot, turn, first=False):
                act.wait_ge(weight_loaded[slot], turn)
                if not first:
                    act.wait_ge(tile_done, t - (RING - 1))
                act.copy(w_hi[:, slot], w_raw[:, slot]).then_inc(hi_ready, 1)

            def split_s(t):
                if t < T_END:
                    split(t, t % RING, 16 * (t // RING + 1), first=t < RING)

            def split_r(i, per, t0, u):
                split(i * per + (t0 + u), u % RING, i * (16 * per // RING) + 16 * ((t0 + u) // RING + 1))

            def rms_root(norm):
                act.wait_ge(mean_ready, norm + 1)
                act.activation(stat[:, 8:10], stat[:, 8:10], ACT.Sqrt).then_inc(root_ready, 1)

            def h_heads(norm):
                for kp in range(KC // 2):
                    act.wait_ge(modulated_ready, 8 * norm + kp + 1)
                    act.copy(h_hi[:, 2 * kp:2 * kp + 2, :], modulated[:, kp % 2]).then_inc(h_hi_ready, 1)

            for dst, src in ((vec_rows[0:KC], c.rearrange("b (r q) -> (b r) q", q=P)),
                             (vec_rows[KC:2 * KC], norm1_w.rearrange("b (r q) -> (b r) q", q=P)),
                             (vec_rows[2 * KC:3 * KC], norm2_w.rearrange("b (r q) -> (b r) q", q=P)),
                             (vec_rows[3 * KC:3 * KC + HH], hgrn_norm_w.rearrange("b (r q) -> (b r) q", q=P)),
                             (bada_rows[:], b_ada.rearrange("b (r q) -> (b r) q", q=P))):
                act.dma_start(dst, src).then_inc(vec_loaded, 16)
            act.dma_start(sink[:], attn_sinks[0].partition_broadcast(P)).then_inc(sink_loaded, 16)
            act.dma_start(low[:], lower_bounds.partition_broadcast(P)).then_inc(low_loaded, 16)

            act.wait_ge(vec_turned, 1)
            act.activation(c_act[:], misc_ps[:, 2, 0:KC], ACT.Silu)
            act.copy(cols[:], misc_ps[:, 2, KC:3 * KC + HH])
            act.copy(bada[:], misc_ps[:, 2, P:P + 6 * KC]).then_inc(c_ready, 1)
            for m in range(M):
                act.wait_ge(x_loaded[m], 16)
                ins = act.activation(xn[:, m], x_sb[:, m], ACT.Square, accum_out=stat[:, m:m + 1])
                ins.then_inc(squares_ready, 1)
            rms_root(0)
            act.wait_ge(low_step, 1)
            act.activation(low[:], low[:], ACT.Exp).then_inc(low_step, 1)
            for t in range(RING):
                split_s(t)
            h_heads(0)

            def take_in(job):
                act.wait_ge(tile_done, JOB_END[job] + 1)
                kind, half = divmod(job - 3, 2)
                cs = slice(N * half, N * half + N)
                if job == 3:
                    act.wait_ge(qk_turned, 3)
                    act.wait_ge(low_step, 3)
                if job == 7:
                    act.wait_ge(f_ready, 4)
                if job == 9:
                    act.wait_ge(scores_ready, PAIRS)
                for m in range(M):
                    src = acc_ps[:, 2 * pair_of(job) + m]
                    if job < 2:
                        ins = act.copy(k_tok[:, m, N * job:N * job + N], src)
                    elif job == 2:
                        s4 = src[:, 0:4 * DH].rearrange("p (g d) -> p g d", g=4)
                        act.copy(k_dup[:, m, :, 0, :], s4)
                        act.copy(k_dup[:, m, :, 1, :], s4)
                        ins = act.copy(v_att[:, m], src[:, 4 * DH:8 * DH])
                    elif kind == 0:
                        ins = act.activation(g_tok[:, m, cs], src, ACT.Sigmoid)
                    elif kind == 1:
                        ins = act.copy(v_tok[:, m, cs], src)
                    elif kind == 2:
                        ins = act.copy(q_tok[:, m, cs], src)
                    else:
                        ins = act.activation(silu_g[:, m, cs], src, ACT.Silu)
                    ins.then_inc(pair_free[pair_of(job)], 1)

            def att_exp(p):
                act.wait_ge(max_ready, p + 1)
                for a in range(2):
                    act.activation(probs[:, a, 0:P], misc_ps[:, a, 0:P], ACT.Exp,
                                   bias=stat[:, 20 + 2 * a:21 + 2 * a], accum_out=stat[:, 28 + 2 * a:29 + 2 * a])
                    act.activation(probs[:, a, P:3 * P], misc_ps[:, a, P:3 * P], ACT.Exp,
                                   bias=stat[:, 21 + 2 * a:22 + 2 * a], accum_out=stat[:, 29 + 2 * a:30 + 2 * a])
                act.activation(stat[:, 24:28], stat[:, 24:28], ACT.Exp).then_inc(exp_ready, 1)

            def hg_exp(h):
                act.wait_ge(sums_ready, h + 1)
                if h >= 2:
                    act.wait_ge(hg_out_ready, h - 1)
                t = hg[:, h % 2]
                rel = misc_ps[:, 0].rearrange("p (m a t) -> p m a t", m=M, a=2)
                two = lambda i: t[:, i].rearrange("p (m t) -> p m t", m=M)
                act.activation(two(0), rel[:, :, 0], ACT.Exp)
                act.activation(two(1), rel[:, :, 0], ACT.Exp, scale=-1.0)
                act.activation(two(2), rel[:, :, 1], ACT.Exp)
                act.activation(t[:, 3], small_ps[:, 0:S], ACT.Exp).then_inc(hg_exp_ready, 1)

            def hg_take(h):
                act.wait_ge(hg_out_ready, h + 1)
                src = misc_ps[:, 2, 0:S].rearrange("p (m t) -> p m t", m=M)
                act.copy(k_tok[:, :, h * P:(h + 1) * P], src)
                if h:
                    act.wait_ge(hg_out_taken, h)
                for m in range(M):
                    ins = act.activation(junk[:, m], misc_ps[:, 2, m * P:(m + 1) * P], ACT.Square,
                                         accum_out=stat[:, 32 + m * HH + h:33 + m * HH + h])
                ins.then_inc(hg_out_taken, 1)

            def gate_row_take(n, dst, which):
                act.wait_ge(gate_spread, 4 * which + n + 1)
                act.copy(dst[:, n * N:(n + 1) * N], misc_ps[:, n % 3]).then_inc(gate_row_ready, 1)

            def squares_of(n, count, before):
                act.wait_ge(x_updated, count)
                act.wait_ge(squares_ready, before)
                for m in range(M):
                    ins = act.activation(sq_junk[:, m], x_sb[:, m, n * N:(n + 1) * N], ACT.Square,
                                         accum_out=stat[:, m * 4 + n:m * 4 + n + 1])
                ins.then_inc(squares_ready, 1)

            def gap(g):
                if g in Q_GAPS or g == K_GAP:
                    u = (*Q_GAPS, K_GAP).index(g)
                    act.wait_ge(qk_turned, u + 1)
                    act.wait_ge(bias_stored, 16)
                    for b in range(2):
                        src = misc_ps[:, b].rearrange("p (a t) -> p a t", a=2)
                        if u < 2:
                            ins = act.mul(qT[:, 4 * u + 2 * b:4 * u + 2 * b + 2], src, DH ** -0.5)
                        else:
                            ins = act.copy(kT[:, 2 * b:2 * b + 2], src)
                    ins.then_inc(qk_ready, 1)
                for job, end in JOB_END.items():
                    if end == g and job < NJ:
                        take_in(job)
                if g == JOB_END[4] + 3:
                    act.wait_ge(f_ready, 4)
                    for m in range(M):
                        act.activation(g_tok[:, m], g_tok[:, m], ACT.Ln).then_inc(logf_ready, 1)
                p, s = divmod(g - ATT_GAP, ATT_PERIOD)
                if 0 <= p < PAIRS:
                    if s == 0:
                        att_exp(p)
                    if s == 2:
                        act.wait_ge(probs_turned, p + 1)
                        for a in range(2):
                            ins = act.copy(probsT[:, a], misc_ps[:, a, 0:3 * P])
                        ins.then_inc(probsT_ready, 1)
                    if s == 4:
                        act.wait_ge(o_att_turned, p + 1)
                        act.copy(mixa_hi[:, p], misc_ps[:, 2, 2 * P:4 * P]).then_inc(mixa_hi_ready, 1)
                h, s = divmod(g - HG_GAP, HG_PERIOD)
                if s == 0:
                    if 0 <= h - 1 < HH:
                        hg_take(h - 1)
                    if 0 <= h < HH:
                        hg_exp(h)
                if g == HG_GAP + HG_PERIOD * HH:
                    act.wait_ge(mean_ready, 2)
                    act.activation(stat[:, 32:48], stat[:, 32:48], ACT.Sqrt).then_inc(root_ready, 1)
                for i in range(4):
                    if FIN_GAPS[i] == g:
                        act.wait_ge(hg_turned, i + 1)
                        if i >= 2:
                            act.wait_ge(mixr_lo_ready, i - 1)
                        for j in range(2):
                            h = 2 * i + j
                            ins = act.activation(modulated[:, i % 2, j], misc_ps[:, i % 3, j * S:(j + 1) * S],
                                                 ACT.Copy, scale=cols[:, 2 * KC + h:2 * KC + h + 1])
                        ins.then_inc(mixr_tmp_ready, 1)
                        act.wait_ge(mixr_tmp_ready, i + 1)
                        act.copy(h_hi[:, 2 * i:2 * i + 2], modulated[:, i % 2]).then_inc(mixr_hi_ready, 1)
                    if G1_GAPS[i] == g:
                        gate_row_take(i, gate1_row, 0)
                for job, end in JOB_END.items():
                    if end == g and job >= NJ:
                        squares_of(job - NJ, 2 * (job - NJ) + 2, 2 + job - NJ)

            for t in range(NS):
                split_s(t + LEAD)
                gap(t)
            act.wait_ge(mean_ready, 3)
            act.activation(stat[:, 8:10], stat[:, 8:10], ACT.Sqrt).then_inc(root_ready, 1)
            h_heads(1)

            def hidden_head(it, dst0):
                for b in range(2):
                    act.wait_ge(hid_turned, it * 2 + (b + 1))
                    act.copy(hid_hi[:, bass.ds(dst0 + 2 * b, 2), :],
                             misc_ps[:, b].rearrange("p (a t) -> p a t", a=2)).then_inc(hid_hi_ready, 1)

            def gate_up(i, t0, job0, before, peeled):
                for u in range(2 * JOB_TILES):
                    split_r(i, 2 * JOB_TILES, t0, u + LEAD)
                    if u == 2 and not peeled:
                        hidden_head(i + (before - 1), i * 4 - 4)
                    if u == JOB_TILES - 1:
                        act.wait_ge(tile_done, i * (2 * JOB_TILES) + (t0 + JOB_TILES))
                        act.wait_ge(hid_t_ready, i * 2 + 2 * before)
                        for m in range(M):
                            act.activation(hid_g[:, m], acc_ps[:, 2 * pair_of(job0) + m],
                                           ACT.Silu).then_inc(hid_g_ready, 1)
                        act.wait_ge(hid_g_ready, i * 2 + (2 * before + 2))
                        act.sem_inc(pair_free[pair_of(job0)], 2)

            gate_up(0, T_GA, JOB_GA, 0, True)
            with act.Fori(1, FA) as i:
                gate_up(i, T_GA, JOB_GA, 0, False)
            hidden_head(FA - 1, 4 * FA - 4)
            for n in range(4):
                gate_row_take(n, gate_row, 1)
            with act.Fori(0, OUT_JOBS // 2) as i:
                for u in range(2 * DT_A):
                    split_r(i, 2 * DT_A, T_DA, u + LEAD)
            gate_up(0, T_GB, JOB_GB, FA, True)
            with act.Fori(1, FB) as i:
                gate_up(i, T_GB, JOB_GB, FA, False)
            hidden_head(FJ - 1, 4 * FB - 4)
            for t in range(T_DB, T_END):
                split_s(t + LEAD)
                n, v = divmod(t - T_DB, DT_B)
                if v == DT_B - 1:
                    squares_of(n, 2 * (2 * OUT_JOBS + n) + 2, 6 + n)
            act.wait_ge(mean_ready, 4)
            act.activation(stat[:, 8:10], stat[:, 8:10], ACT.Sqrt).then_inc(root_ready, 1)

        @block.vector
        def _(dve):
            chain = [0]

            def link(ins):
                chain[0] += 1
                ins.then_inc(dve_chain, 1)
                dve.wait_ge(dve_chain, chain[0])

            def split(t, slot):
                dve.wait_ge(hi_ready, t + 1)
                dve.tensor_tensor(w_lo[:, slot], w_raw[:, slot], w_hi[:, slot].bitcast(F32),
                                  ALU.subtract).then_inc(lo_ready, 1)

            def split_s(t):
                if t < T_END:
                    split(t, t % RING)

            def add_ada(slot, turn, count, buf, ccol, first, last):
                dve.wait_ge(ada_loaded[slot], turn)
                if first:
                    ins = dve.tensor_scalar(acc[:, buf], ada[:, slot], ccol, None, ALU.mult)
                else:
                    dve.wait_ge(ada_on_dve, count)
                    ins = dve.scalar_tensor_tensor(acc[:, buf], ada[:, slot], ccol, acc[:, buf],
                                                   ALU.mult, ALU.add)
                ins.then_inc(ada_on_dve, 1)
                return ins

            def mean_root(norm, parts):
                if parts:
                    for m in range(M):
                        ins = dve.tensor_reduce(stat[:, 10 + m:11 + m], stat[:, 4 * m:4 * m + 4], AX.X, ALU.add)
                    link(ins)
                    src = stat[:, 10:12]
                else:
                    src = stat[:, 0:2]
                dve.tensor_scalar(stat[:, 8:10], src, 1.0 / D, EPS, ALU.mult, ALU.add).then_inc(mean_ready, 1)

            def normalise(norm, roots):
                dve.wait_ge(root_ready, roots)
                link(dve.reciprocal(stat[:, 12:14], stat[:, 8:10]))
                for m in range(M):
                    dve.tensor_scalar(xn[:, m], x_sb[:, m], stat[:, 12 + m:13 + m], None,
                                      ALU.mult).then_inc(xn_ready, 1)

            def modulate(norm):
                shift, scale = (SHIFT1, SCALE1) if norm == 0 else (SHIFT2, SCALE2)
                link(dve.tensor_scalar(gain[:], mod[:, scale:scale + KC], 1.0, None, ALU.add))
                link(dve.tensor_tensor(gain[:], gain[:], cols[:, norm * KC:(norm + 1) * KC], ALU.mult))

                def tail(kp):
                    dve.wait_ge(h_hi_ready, 8 * norm + kp + 1)
                    dve.tensor_tensor(h_lo[:, 2 * kp:2 * kp + 2], modulated[:, kp % 2],
                                      h_hi[:, 2 * kp:2 * kp + 2].bitcast(F32),
                                      ALU.subtract).then_inc(h_lo_ready, 1)

                for kp in range(KC // 2):
                    dve.wait_ge(xn_turned, 8 * norm + kp + 1)
                    if kp >= 2:
                        dve.wait_ge(h_lo_ready, 8 * norm + kp - 1)
                    for j in range(2):
                        kc = 2 * kp + j
                        ins = dve.tensor_scalar(modulated[:, kp % 2, j], misc_ps[:, kp % 2, j * S:(j + 1) * S],
                                                gain[:, kc:kc + 1], mod[:, shift + kc:shift + kc + 1],
                                                ALU.mult, ALU.add)
                    ins.then_inc(modulated_ready, 1)
                    if kp:
                        tail(kp - 1)
                tail(KC // 2 - 1)

            dve.wait_ge(c_ready, 1)
            dve.wait_ge(squares_ready, 2)
            mean_root(0, False)

            def ada_block(i, b):
                if b is None:
                    return
                for kc in range(1, KC, 2):
                    n = 8 * b + kc // 2
                    if kc == 1:
                        dve.wait_ge(block_reduced, i * 2 + (b - 1)) if b == 1 else None
                    ins = add_ada(kc % RING, i * (16 * 8) + 16 * (4 * b + kc // 4 + 1),
                                  i * 16 + n, b, c_act[:, kc:kc + 1], kc == 1, False)
                dve.wait_ge(ada_on_dve, i * 16 + (8 * b + 8))
                dve.sem_inc(block_summed, 1)

            def low_bounds():
                dve.wait_ge(low_loaded, 16)
                link(dve.tensor_tensor(low_t[:], low[:, 0], low[:, 1], ALU.max))
                for j in range(2):
                    ins = dve.tensor_tensor(low[:, j], low[:, j], low_t[:], ALU.subtract)
                ins.then_inc(low_step, 1)

            ada_block(0, 0)
            ada_block(0, 1)
            normalise(0, 1)
            low_bounds()
            dve.wait_ge(block_reduced, 2)
            ada_block(1, 0)
            ada_block(1, 1)
            dve.wait_ge(low_step, 2)
            link(dve.tensor_tensor(low_t[:], low[:, 0], low[:, 1], ALU.add))
            link(dve.reciprocal(low_t[:], low_t[:]))
            for j in range(2):
                ins = dve.tensor_tensor(low[:, j], low[:, j], low_t[:], ALU.mult)
            ins.then_inc(low_step, 1)
            dve.wait_ge(block_reduced, 4)
            link(dve.tensor_tensor(mod[:, 0:2 * KC], small_ps[:, 0:2 * KC], bada[:, 0:2 * KC], ALU.add))
            dve.sem_inc(mod_ready, 1)
            for t in range(RING):
                split_s(t)
            modulate(0)

            def ada_s(t):
                if t >= ADA_STRAIGHT:
                    return
                a = ADA_0 + t
                turn = 16 * (a // RING + 1)
                if t < 6 * KC:
                    q, kc = 4 + t // KC, t % KC
                    first, last, buf = kc == 0, kc == KC - 1, q % 2
                    if first:
                        dve.wait_ge(block_reduced, q - 1)
                else:
                    kc, buf = divmod(t - 6 * KC, 2)
                    first, last = kc == 0, False
                    if first:
                        dve.wait_ge(block_reduced, 9 + buf)
                add_ada(a % RING, turn, ADA_0 // 2 + t, buf, c_act[:, kc:kc + 1], first, last)
                if last:
                    dve.wait_ge(ada_on_dve, ADA_0 // 2 + t + 1)
                    dve.sem_inc(block_summed, 1)

            def att_max(p):
                dve.wait_ge(scores_ready, p + 1)
                top = stat[:, 16:20].rearrange("p (a m) -> p a m", a=2)
                dve.tensor_reduce(top[:, :, 0], misc_ps[:, 0:2, 0:P], AX.X, ALU.max)
                link(dve.tensor_reduce(top[:, :, 1], misc_ps[:, 0:2, P:3 * P], AX.X, ALU.max))
                sk = sink[:, 2 * p:2 * p + 2].unsqueeze(2).to_broadcast([P, 2, 2])
                link(dve.tensor_tensor(top, top, sk, ALU.max))
                dve.tensor_scalar(stat[:, 20:24], stat[:, 16:20], -1.0, None, ALU.mult)
                dve.tensor_tensor(stat[:, 24:28].rearrange("p (a m) -> p a m", a=2), sk, top,
                                  ALU.subtract).then_inc(max_ready, 1)

            def att_den(p):
                dve.wait_ge(exp_ready, p + 1)
                link(dve.tensor_tensor(stat[:, 28:32], stat[:, 28:32], stat[:, 24:28], ALU.add))
                link(dve.reciprocal(stat[:, 28:32], stat[:, 28:32]))

            def att_out(p):
                dve.wait_ge(pv_ready, p + 1)
                rden = stat[:, 28:32].rearrange("p (a m) -> p m a", a=2).unsqueeze(3).to_broadcast([P, M, 2, DH])
                dve.tensor_tensor(o_att[:].rearrange("p m (a d) -> p m a d", a=2),
                                  misc_ps[:, 2, 0:S].rearrange("p (m a d) -> p m a d", m=M, a=2),
                                  rden, ALU.mult).then_inc(o_att_ready, 1)

            def hg_ops(h):
                t = hg[:, h % 2]
                hc = slice(h * P, (h + 1) * P)
                dve.wait_ge(hg_exp_ready, h + 1)
                link(dve.tensor_copy(decay[:], t[:, 2].rearrange("p (c t) -> p c t", c=4)[:, :, CH - 1]))
                q, k = misc_ps[:, 1, 0:S], misc_ps[:, 1, S:2 * S]
                dve.tensor_tensor(t[:, 0], q, t[:, 0], ALU.mult)
                dve.tensor_tensor(t[:, 1], k, t[:, 1], ALU.mult)
                dve.tensor_tensor(t[:, 2], q, t[:, 2], ALU.mult)
                t3 = t[:, 3].rearrange("p (m t) -> p m t", m=M)
                dve.tensor_tensor(t3, k_tok[:, :, hc], t3, ALU.mult).then_inc(hg_ops_ready, 1)

            def hg_state(h):
                dve.wait_ge(hg_scores_ready, h + 1)
                for m in range(M):
                    dve.copy_predicated(att[:, m], upper[:, 1].bitcast(I32), misc_ps[:, 2, m * P:(m + 1) * P])
                link(dve.tensor_copy(state[:, 0], misc_ps[:, 2, S:S + P]))
                link(dve.scalar_tensor_tensor(state[:, 1], state[:, 0], decay[:, 1:2],
                                              misc_ps[:, 0, 0:P], ALU.mult, ALU.add))
                dve.scalar_tensor_tensor(state[:, 2], state[:, 1], decay[:, 2:3],
                                         misc_ps[:, 2, S + P:S + 2 * P],
                                         ALU.mult, ALU.add).then_inc(hg_state_ready, 1)

            def hg_norm():
                dve.wait_ge(hg_out_taken, HH)
                dve.tensor_scalar(stat[:, 32:48], stat[:, 32:48], 1.0 / P, EPS,
                                  ALU.mult, ALU.add).then_inc(mean_ready, 1)
                dve.wait_ge(root_ready, 2)
                link(dve.reciprocal(stat[:, 48:64], stat[:, 32:48]))
                dve.wait_ge(pair_free[pair_of(10)], job_free_count(10) + 2)
                dve.wait_ge(pair_free[pair_of(9)], job_free_count(9) + 2)
                for h in range(HH):
                    for m in range(M):
                        hc = slice(h * P, (h + 1) * P)
                        ins = dve.scalar_tensor_tensor(k_tok[:, m, hc], k_tok[:, m, hc],
                                                       stat[:, 48 + m * HH + h:49 + m * HH + h],
                                                       silu_g[:, m, hc], ALU.mult, ALU.mult)
                ins.then_inc(hg_normed, 1)

            def take_gated(job, n0, row, end, count, col):
                dve.wait_ge(tile_done, end)
                dve.wait_ge(x_updated, count * 2)
                for m in range(M):
                    dve.tensor_tensor(gated[:, m], acc_ps[:, 2 * pair_of(job) + m], row[:, bass.ds(col, N)],
                                      ALU.mult).then_inc(pair_free[pair_of(job)], 1)
                dve.wait_ge(pair_free[pair_of(job)], n0)
                for m in range(M):
                    xs = x_sb[:, m, bass.ds(col, N)]
                    dve.tensor_tensor(xs, xs, gated[:, m], ALU.add).then_inc(x_updated, 1)

            def gap(g):
                if g in RED_GAP:
                    q = RED_GAP[g]
                    dve.wait_ge(block_reduced, q + 1)
                    dve.tensor_tensor(mod[:, 8 * q:8 * q + 8], small_ps[:, 8 * q:8 * q + 8],
                                      bada[:, 8 * q:8 * q + 8], ALU.add).then_inc(mod_ready, 1)
                p, s = divmod(g - ATT_GAP, ATT_PERIOD)
                if 0 <= p < PAIRS:
                    if s == 0:
                        if p == 0:
                            dve.wait_ge(sink_loaded, 16)
                        att_max(p)
                    if s == 2:
                        att_den(p)
                    if s == 3:
                        att_out(p)
                    if s == 4:
                        dve.wait_ge(mixa_hi_ready, p + 1)
                        dve.tensor_tensor(mixa_lo[:, p], misc_ps[:, 2, 2 * P:4 * P], mixa_hi[:, p].bitcast(F32),
                                          ALU.subtract).then_inc(mixa_lo_ready, 1)
                h, s = divmod(g - HG_GAP, HG_PERIOD)
                if 0 <= h < HH:
                    if s == 0:
                        hg_ops(h)
                    if s == 2:
                        hg_state(h)
                if g == HG_GAP + HG_PERIOD * HH:
                    hg_norm()
                for i in range(4):
                    if FIN_GAPS[i] == g:
                        dve.wait_ge(mixr_hi_ready, i + 1)
                        dve.tensor_tensor(h_lo[:, 2 * i:2 * i + 2], modulated[:, i % 2],
                                          h_hi[:, 2 * i:2 * i + 2].bitcast(F32),
                                          ALU.subtract).then_inc(mixr_lo_ready, 1)
                for job, end in JOB_END.items():
                    if end == g and job >= NJ:
                        dve.wait_ge(gate_row_ready, 4)
                        take_gated(job, job_free_count(job) + 2, gate1_row, end + 1, job - NJ, (job - NJ) * N)

            dve.wait_ge(consts_ready, 1)
            for t in range(NS):
                split_s(t + LEAD)
                ada_s(t + LEAD) if t else [ada_s(u) for u in range(LEAD + 1)]
                gap(t)
            dve.wait_ge(squares_ready, 6)
            mean_root(1, True)
            normalise(1, 3)
            modulate(1)

            def hidden_tail(it, dst0):
                for b in range(2):
                    dve.wait_ge(hid_hi_ready, it * 2 + (b + 1))
                    dst = bass.ds(dst0 + 2 * b, 2)
                    dve.tensor_tensor(hid_lo[:, dst, :], misc_ps[:, b].rearrange("p (a t) -> p a t", a=2),
                                      hid_hi[:, dst, :].bitcast(F32), ALU.subtract).then_inc(hid_lo_ready, 1)

            def gate_up(i, t0, job0, before, peeled):
                for u in range(2 * JOB_TILES):
                    split(i * (2 * JOB_TILES) + (t0 + u + LEAD), u % RING)
                    if before == 0 and u % 4 == 3:
                        v = u // 4
                        a = ADA_0 + ADA_STRAIGHT
                        add_ada(v, i * 16 + 16 * (a // RING + 1), i * 4 + (ADA_0 // 2 + ADA_STRAIGHT + v),
                                v % 2, c_act[:, bass.ds(i * 2 + (ADA_G2_STRAIGHT // 2 + v // 2), 1)], False, False)
                    if u == 2 and not peeled:
                        hidden_tail(i + (before - 1), i * 4 - 4)
                    if u == 2 * JOB_TILES - 1:
                        dve.wait_ge(tile_done, i * (2 * JOB_TILES) + (t0 + 2 * JOB_TILES))
                        dve.wait_ge(hid_g_ready, i * 2 + (2 * before + 2))
                        dve.wait_ge(hid_turned, i * 2 + 2 * before)
                        for m in range(M):
                            dve.tensor_tensor(hid_t[:, m], acc_ps[:, 2 * pair_of(job0 + 1) + m], hid_g[:, m],
                                              ALU.mult).then_inc(hid_t_ready, 1)
                        dve.wait_ge(hid_t_ready, i * 2 + (2 * before + 2))
                        dve.sem_inc(pair_free[pair_of(job0 + 1)], 2)

            def down(i, t0, job0, tiles, before):
                for u in range(2 * tiles):
                    if isinstance(i, int):
                        split_s(t0 + 2 * tiles * i + u + LEAD)
                    else:
                        split(i * (2 * tiles) + (t0 + u + LEAD), u % RING)
                    jj, v = divmod(u, tiles)
                    if v == tiles - 1:
                        job = job0 + jj
                        take_gated(job, i * 2 + (job_free_count(job) + 2), gate_row,
                                   i * (2 * tiles) + (t0 + (jj + 1) * tiles), i * 2 + (before + jj),
                                   i * (2 * N) + jj * N)

            gate_up(0, T_GA, JOB_GA, 0, True)
            with dve.Fori(1, FA) as i:
                gate_up(i, T_GA, JOB_GA, 0, False)
            dve.wait_ge(ada_on_dve, ADA_0 // 2 + ADA_STRAIGHT + 4 * FA)
            dve.sem_inc(block_summed, 2)
            hidden_tail(FA - 1, 4 * FA - 4)
            dve.wait_ge(block_reduced, 12)
            dve.tensor_tensor(mod[:, GATE2:GATE2 + KC], small_ps[:, GATE2:GATE2 + KC],
                              bada[:, GATE2:GATE2 + KC], ALU.add).then_inc(mod_ready, 1)
            dve.wait_ge(gate_row_ready, 8)
            with dve.Fori(0, OUT_JOBS // 2) as i:
                down(i, T_DA, JOB_DA, DT_A, OUT_JOBS)
            gate_up(0, T_GB, JOB_GB, FA, True)
            with dve.Fori(1, FB) as i:
                gate_up(i, T_GB, JOB_GB, FA, False)
            hidden_tail(FJ - 1, 4 * FB - 4)
            for i in range(OUT_JOBS // 2):
                down(i, T_DB, JOB_DB, DT_B, 2 * OUT_JOBS)
            dve.wait_ge(squares_ready, 10)
            mean_root(2, True)
            dve.wait_ge(root_ready, 4)
            link(dve.reciprocal(stat[:, 12:14], stat[:, 8:10]))
            dve.wait_ge(final_loaded, 16)
            for q in range(4):
                m, half = divmod(q, 2)
                hs = slice(half * AC, (half + 1) * AC)
                dve.scalar_tensor_tensor(y_sb[:, m, hs], x_sb[:, m, hs], stat[:, 12 + m:13 + m],
                                         final_row[:, hs], ALU.mult, ALU.mult).then_inc(y_ready, 1)

        @block.gpsimd
        def _(pool):
            chain = [0]

            def link(ins):
                chain[0] += 1
                ins.then_inc(pool_chain, 1)
                pool.wait_ge(pool_chain, chain[0])

            def keep(ap, pattern, base, mult, op=ALU.is_ge, fill=0.0):
                link(pool.affine_select(out=ap, in_=ap, compare_op=op, fill=fill, base=base,
                                        pattern=pattern, channel_multiplier=mult))

            up, rel = upper[:, 1], upper[:, 0]
            pool.memset(ones[:], 1.0)
            link(pool.memset(ident[:], 0.0))
            keep(ident[:], [[-1, P]], 0, 1, ALU.not_equal, 1.0)
            link(pool.memset(flip[:], 0.0))
            keep(flip[:], [[1, P]], 1 - P, 1, ALU.not_equal, 1.0)
            link(pool.memset(upper[:], 1.0))
            keep(up, [[1, P]], 0, -1)
            keep(up[:, CH:P], [[0, CH]], -CH, 1)
            keep(rel[:, 0:CH], [[0, CH]], CH // 2 - 1, -1)
            keep(rel[:, CH:P], [[0, CH]], -CH, 1)
            keep(rel[:, CH:P], [[0, CH]], CH + CH // 2 - 1, -1)
            link(pool.tensor_tensor(rel, up, rel, ALU.subtract))
            link(pool.memset(after[:], 1.0))
            keep(after[:], [[-1, P]], 0, 1, ALU.is_gt)
            keep(after[:, 0:CH], [[0, CH]], CH - 1, -1)
            link(pool.memset(att[:], 0.0))
            pool.sem_inc(consts_ready, 1)

            pool.dma_start(table_t[:], rel_bias_table.rearrange("b h -> h b"),
                           allow_slow_non_contiguous=True).then_inc(table_loaded, 16)
            link(pool.memset(bias_row[:], NEG))
            pool.wait_ge(table_loaded, 16)
            for b, (lo, hi) in enumerate(bucket_ranges()):
                if lo > hi:
                    continue
                n = hi - lo + 1
                ins = pool.tensor_copy(bias_row[:, 2 * P - 1 - hi:2 * P - lo],
                                       table_t[:, b:b + 1].to_broadcast([AH, n]))
            link(ins)
            pool.dma_start(bias_dram, bias_row[:]).then_inc(bias_stored, 16)
            pool.wait_ge(bias_stored, 16)

            def load_bias(h):
                if h >= 4:
                    pool.wait_ge(scores_ready, (h - 4) // 2 + 1)
                pool.dma_start(bias[:, h % 4], bass.AP(bias_dram.tensor, h * 3 * P, [[1, P], [1, 2 * P]])
                               ).then_inc(bias_loaded[h % 4], 16)

            for h in range(4):
                load_bias(h)
            for half in range(2):
                cs = slice(half * N, half * N + N)
                if half == 0:
                    load_bias(4)
                    load_bias(5)
                job = 3 + half
                pool.wait_ge(pair_free[pair_of(job)], job_free_count(job) + 2)
                for m in range(M):
                    link(pool.tensor_tensor(k_tok[:, m, cs], g_tok[:, m, cs], low[:, 1, cs], ALU.mult))
                    link(pool.tensor_tensor(g_tok[:, m, cs], k_tok[:, m, cs], low[:, 0, cs], ALU.add))
                    pool.tensor_scalar(k_tok[:, m, cs], g_tok[:, m, cs], -1.0, 1.0, ALU.mult,
                                       ALU.add).then_inc(f_ready, 1)
            for h in range(6, AH):
                load_bias(h)


def bucket_ranges():
    import numpy as np
    half = REL_BUCKETS // 2
    d = np.arange(REL_MAX)
    log_b = half + (np.log(np.maximum(d, 1) / half) / np.log(REL_MAX / half)
                    * (REL_BUCKETS - half)).astype(np.int32)
    b = np.where(d < half, d, np.minimum(log_b, REL_BUCKETS - 1))
    out = []
    for i in range(REL_BUCKETS):
        w = np.nonzero(b == i)[0]
        out.append((int(w[0]), int(w[-1])) if len(w) else (1, 0))
    return out


_INS = ["x", "c", "w_ada", "b_ada", "norm1_w", "w_in", "lower_bounds", "hgrn_norm_w", "attn_sinks",
        "rel_bias_table", "w_out", "norm2_w", "w_gate", "w_up", "w_down", "final_norm_w"]


def kernel(**inputs):
    import numpy as _np
    import concourse.bacc as _bacc
    from concourse import mybir as _mybir
    from concourse.bass_utils import run_bass_kernel_spmd as _run

    nc = _bacc.Bacc("TRN2", target_bir_lowering=False, num_devices=1)
    arrays, args = {}, []
    for name in _INS:
        a = _np.ascontiguousarray(inputs[name])
        arrays[f"in_{name}"] = a
        args.append(nc.dram_tensor(f"in_{name}", a.shape, _mybir.dt.from_np(a.dtype), kind="ExternalInput").ap())
    args.append(nc.dram_tensor("out", (1, S, D), F32, kind="ExternalOutput").ap())
    build(nc, *args)
    r = _run(nc, [arrays], core_ids=[0])
    return r.results[0]["out"]
```

```python
from contextlib import ExitStack

import concourse.bass as bass
import concourse.mybir as mybir

ALU = mybir.AluOpType
ACT = mybir.ActivationFunctionType
AX = mybir.AxisListType
F32 = mybir.dt.float32
F32R = mybir.dt.float32r
I32 = mybir.dt.int32

P = 128
D = 2048
S = 256
M = S // P
KC = D // P
N = 512
TK = 2
RING = 4
RING_0 = 8
LEAD = RING
HW = 1024
HH = HW // P
CH = 64
AH = 16
DH = 64
PAIRS = AH // 2
REL_BUCKETS, REL_MAX = 32, 128
F = 5632
FJ = F // N
FA = 6
FB = FJ - FA
EPS = 1e-6
NEG = -1e30

IN_COLS = [4096, 4608, 5120, 1024, 1536, 2048, 2560, 0, 512, 3072, 3584]
NJ = len(IN_COLS)
JOB_TILES = KC // TK
QJ = 3
QUARTERS = 4
QT = JOB_TILES // QUARTERS
STRAIGHT = [(j, TK * (QT * q + i), q == 0 and i == 0, q == QUARTERS - 1 and i == QT - 1)
            for q in range(QUARTERS) for j in range(QJ) for i in range(QT)]
Q_TILES = len(STRAIGHT)
STRAIGHT += [(j, TK * i, i == 0, i == JOB_TILES - 1) for j in range(QJ, NJ) for i in range(JOB_TILES)]
HALF = JOB_TILES // 2
for half in (1, 0):
    for n in (0, 1):
        STRAIGHT += [(NJ + n, TK * (HALF * half + i), half == 1 and i == 0, half == 0 and i == HALF - 1)
                     for i in range(HALF)]
for n in (2, 3):
    STRAIGHT += [(NJ + n, TK * i, i == 0, i == JOB_TILES - 1) for i in range(JOB_TILES)]
NS = len(STRAIGHT)
JOB_END = {j: t for t, (j, _, _, last) in enumerate(STRAIGHT) if last}
OUT_JOBS = D // N
J_FFN = NJ + OUT_JOBS
T_GA = NS
T_DA = T_GA + 2 * JOB_TILES * FA
DT_A = FA * 4 // TK
T_GB = T_DA + OUT_JOBS * DT_A
T_DB = T_GB + 2 * JOB_TILES * FB
DT_B = FB * 4 // TK
T_END = T_DB + OUT_JOBS * DT_B
JOB_GA = J_FFN
JOB_DA = JOB_GA + 2 * FA
JOB_GB = JOB_DA + OUT_JOBS
JOB_DB = JOB_GB + 2 * FB

AC = 1024
ADA_0 = 4 * KC
ADA_STRAIGHT = 6 * KC
MIX_AT = (1, 4, 6, 9, 11, 14)
assert len(MIX_AT) == QJ * QT


PE_EVERY = 4
ADA_0_DVE = ADA_0 - ADA_0 // PE_EVERY


def ada_slot(a):
    return a % RING_0 if a < ADA_0 else a % RING


def ada_turn(a):
    return 16 * (a // RING_0 + 1) if a < ADA_0 else 16 * (ADA_0 // RING_0 + (a - ADA_0) // RING + 1)


def ada_before(n):
    return n // 2 if n < 8 else min(n - 4 + max(0, n - 9) // 6, ADA_STRAIGHT)


def ada_beside(t):
    n = t - Q_TILES
    if n < 0:
        return ()
    return tuple(range(ada_before(n), ada_before(n + 1)))


def gate2_peeled(u):
    if u < 0:
        return ()
    if u < LEAD:
        return (2 * u, 2 * u + 1)
    return (u + LEAD,) if u + LEAD < 2 * JOB_TILES else ()


GATE2_LOOP = (0, 4, 8, 11)
G2_0 = ADA_0 + ADA_STRAIGHT
G2_LOOP = ADA_0_DVE + ADA_STRAIGHT + 2 * JOB_TILES - 4
SHIFT1, SCALE1, GATE1, SHIFT2, SCALE2, GATE2 = (KC * i for i in range(6))

LOW_GAPS = (20, 23, 26)
Q_GAPS = (25, 27)
K_GAP = 29
ATT_GAP, ATT_PERIOD = 31, 4
HG_GAP, HG_PERIOD = 65, 3
FIN_GAPS = (92, 93, 94, 94)
G1_GAPS = (97, 97, 98, 98)
RED_GAP = {41: 4, 54: 5, 67: 6, 81: 7, 96: 8, 110: 9}
SUMS_BEFORE = {6: 1, 7: 6}


def build(nc, x, c, w_ada, b_ada, norm1_w, w_in, lower_bounds, hgrn_norm_w, attn_sinks,
          rel_bias_table, w_out, norm2_w, w_gate, w_up, w_down, final_norm_w, out):
    ctx = ExitStack()
    with ctx:
        base = (nc.sbuf_base + 31) // 32 * 32
        at = [base]

        def sb(name, shape, dt=F32, offset=None):
            size = 4
            for n in shape[1:]:
                size *= n
            if offset is None:
                offset = at[0]
                at[0] += (size + 31) // 32 * 32
            assert offset + size <= nc.sbuf_usable_end, (name, offset + size - nc.sbuf_usable_end)
            return nc.alloc_sbuf_tensor_at(name, shape, dt, offset=offset)

        def sem(name):
            return ctx.enter_context(nc.semaphore(name))

        x_sb = sb("x_sb", [P, M, D])
        h_hi = sb("h_hi", [P, KC, S], F32R)
        h_lo_at = at[0]
        h_lo = sb("h_lo", [P, KC, S], F32R)
        w_raw = sb("w_raw", [P, RING, TK, N])
        w_hi = sb("w_hi", [P, RING, TK, N], F32R)
        w_lo = sb("w_lo", [P, RING, TK, N], F32R)
        ada = sb("ada", [P, RING, AC])
        acc = sb("acc", [P, 2, AC])
        ident = sb("ident", [P, P])
        upper = sb("upper", [P, 2, P])
        after = sb("after", [P, P])
        ones = sb("ones", [P, 1])
        minus_half = sb("minus_half", [P, 2 * HH])
        flip = sb("flip", [P, P])
        c_act = sb("c_act", [P, KC])
        cols = sb("cols", [P, 2 * KC + HH])
        bada = sb("bada", [P, 6 * KC])
        mod = sb("mod", [P, 6 * KC])
        gain = sb("gain", [P, KC])
        sink = sb("sink", [P, AH])
        stat = sb("stat", [P, 64])
        decay = sb("decay", [P, 4])
        mix_hi_at = at[0]
        ada_more = sb("ada_more", [P, RING_0 - RING, AC], offset=mix_hi_at)
        mixa_hi = sb("mixa_hi", [P, HH, S], F32R)
        mixa_lo = sb("mixa_lo", [P, HH, S], F32R)
        work = at[0]
        KB = 1024
        k_tok = sb("k_tok", [P, M, HW], offset=work)
        g_tok = sb("g_tok", [P, M, HW], offset=work + 8 * KB)
        v_tok = sb("v_tok", [P, M, HW], offset=work + 16 * KB)
        q_tok = sb("q_tok", [P, M, HW], offset=work + 24 * KB)
        k_dup = sb("k_dup", [P, M, 4, 2, DH], offset=work + 8 * KB)
        low = sb("low", [P, 2, HW], offset=work + 24 * KB)
        low_t = sb("low_t", [P, HW], offset=work + 16 * KB)
        qT = sb("qT", [P, PAIRS, S], offset=work + 32 * KB)
        silu_g = sb("silu_g", [P, M, HW], offset=work + 32 * KB)
        kT = sb("kT", [P, 4, S], offset=work + 40 * KB)
        v_att = sb("v_att", [P, M, 4 * DH], offset=work + 44 * KB)
        o_att = sb("o_att", [P, M, P], offset=work + 46 * KB)
        bias = sb("bias", [P, 4, 2 * P], offset=work + 47 * KB)
        probs = sb("probs", [P, 2, 3 * P], offset=work + 51 * KB)
        probsT = sb("probsT", [P, 2, 3 * P], offset=work + 54 * KB)
        gated = sb("gated", [P, M, N], offset=work + 51 * KB)
        hg = sb("hg", [P, 2, 4, S], offset=work + 57 * KB)
        modulated = sb("modulated", [P, 2, 2, S], offset=work + 57 * KB)
        state = sb("state", [P, 3, P], offset=work + 65 * KB)
        att = sb("att", [P, M, P], offset=work + 65 * KB + 1536)
        junk = sb("junk", [P, M, P], offset=work + 44 * KB)
        table_t = sb("table_t", [AH, REL_BUCKETS], offset=work + 32 * KB)
        bias_row = sb("bias_row", [AH, 3 * P], offset=work + 33 * KB)
        vec_rows = sb("vec_rows", [3 * KC + HH, P], offset=work + 16 * KB)
        bada_rows = sb("bada_rows", [6 * KC, P], offset=work + 17 * KB)
        xn = sb("xn", [P, M, D], offset=work)
        sq_junk = sb("sq_junk", [P, M, N], offset=work + 57 * KB)
        hid_hi = sb("hid_hi", [P, 4 * FA, S], F32R, offset=mix_hi_at)
        hid_lo = sb("hid_lo", [P, 4 * FA, S], F32R, offset=mix_hi_at + 24 * KB)
        hid_g = sb("hid_g", [P, M, N], offset=work + 32 * KB)
        hid_t = sb("hid_t", [P, M, N], offset=work + 36 * KB)
        gate_row = sb("gate_row", [P, D], offset=work + 40 * KB)
        gate1_row = sb("gate1_row", [P, D], offset=work + 8 * KB)
        final_row = acc[:].rearrange("p a n -> p (a n)")
        y_sb = sb("y_sb", [P, M, D], offset=h_lo_at)

        def ada_at(slot):
            return ada[:, slot] if slot < RING else ada_more[:, slot - RING]

        acc_ps = ctx.enter_context(nc.psum_tensor("acc_ps", [P, 4, N], F32))
        small_ps = ctx.enter_context(nc.psum_tensor("small_ps", [P, N], F32))
        misc_ps = ctx.enter_context(nc.psum_tensor("misc_ps", [P, 3, N], F32))

        bias_dram = nc.dram_tensor("bias_dram", (AH, 3 * P), F32, kind="Internal").ap()

        x_loaded = [sem(f"x_loaded{m}") for m in range(M)]
        vec_loaded = sem("vec_loaded")
        sink_loaded = sem("sink_loaded")
        low_loaded = sem("low_loaded")
        table_loaded = sem("table_loaded")
        bias_stored = sem("bias_stored")
        bias_loaded = [sem(f"bias_loaded{i}") for i in range(4)]
        final_loaded = sem("final_loaded")
        weight_loaded = [sem(f"weight_loaded{i}") for i in range(RING)]
        ada_loaded = [sem(f"ada_loaded{i}") for i in range(RING_0)]
        out_stored = sem("out_stored")

        consts_ready = sem("consts_ready")
        pool_chain = sem("pool_chain")
        act_chain = sem("act_chain")
        dve_chain = sem("dve_chain")

        hi_ready = sem("hi_ready")
        lo_ready = sem("lo_ready")
        tile_done = sem("tile_done")
        pair_free = [sem(f"pair_free{i}") for i in range(3)]

        vec_turned = sem("vec_turned")
        c_ready = sem("c_ready")
        ada_on_pe = sem("ada_on_pe")
        ada_on_dve = sem("ada_on_dve")
        block_summed = sem("block_summed")
        block_reduced = sem("block_reduced")
        mod_ready = sem("mod_ready")

        squares_ready = sem("squares_ready")
        root_ready = sem("root_ready")
        mean_ready = sem("mean_ready")
        xn_ready = sem("xn_ready")
        xn_turned = sem("xn_turned")
        gain_ready = sem("gain_ready")
        modulated_ready = sem("modulated_ready")
        h_hi_ready = sem("h_hi_ready")
        h_lo_ready = sem("h_lo_ready")

        qk_turned = sem("qk_turned")
        qk_ready = sem("qk_ready")
        low_step = sem("low_step")
        f_ready = sem("f_ready")
        logf_ready = sem("logf_ready")

        scores_ready = sem("scores_ready")
        max_ready = sem("max_ready")
        exp_ready = sem("exp_ready")
        probs_turned = sem("probs_turned")
        probsT_ready = sem("probsT_ready")
        pv_ready = sem("pv_ready")
        o_att_ready = sem("o_att_ready")
        o_att_turned = sem("o_att_turned")
        mixa_hi_ready = sem("mixa_hi_ready")
        mixa_lo_ready = sem("mixa_lo_ready")

        sums_ready = sem("sums_ready")
        hg_exp_ready = sem("hg_exp_ready")
        hg_ops_ready = sem("hg_ops_ready")
        hg_scores_ready = sem("hg_scores_ready")
        hg_state_ready = sem("hg_state_ready")
        hg_out_ready = sem("hg_out_ready")
        hg_out_taken = sem("hg_out_taken")
        hg_normed = sem("hg_normed")
        hg_turned = sem("hg_turned")
        mixr_tmp_ready = sem("mixr_tmp_ready")
        mixr_hi_ready = sem("mixr_hi_ready")
        mixr_lo_ready = sem("mixr_lo_ready")

        gate_spread = sem("gate_spread")
        gate_row_ready = sem("gate_row_ready")
        weighted_ready = sem("weighted_ready")
        x_updated = sem("x_updated")
        hid_g_ready = sem("hid_g_ready")
        hid_t_ready = sem("hid_t_ready")
        hid_turned = sem("hid_turned")
        hid_hi_ready = sem("hid_hi_ready")
        hid_lo_ready = sem("hid_lo_ready")
        y_ready = [sem(f"y_ready{m}") for m in range(M)]

        x_dram = x.rearrange("b (m p) d -> p (b m) d", p=P)
        out_dram = out.rearrange("b (m p) d -> p (b m) d", p=P)
        wada = w_ada[0]

        def chunked(w, k0, nk, c0, n):
            return w[k0 * P:(k0 + nk) * P, bass.ds(c0, n)].rearrange("(c p) n -> p c n", p=P)

        def pair_of(job):
            return job if job < QJ else (job - QJ) % 2

        def bank_of(job, m):
            return misc_ps[:, 1 + m] if pair_of(job) == 2 else acc_ps[:, 2 * pair_of(job) + m]

        def job_free_count(job):
            return 0 if job < QJ else 2 * ((job - QJ) // 2 + 1)

        block = ctx.enter_context(nc.Block())

        @block.sync
        def _(sp):
            def load_weight(t, slot, src, first=False):
                if not first:
                    sp.wait_ge(lo_ready, t - (RING - 1))
                sp.dma_start(w_raw[:, slot], src).then_inc(weight_loaded[slot], 16)

            def load_ada(slot, src):
                dst = ada_at(slot)
                if len(src.shape) == 3:
                    dst = dst.rearrange("p (g n) -> p g n", g=2)
                sp.dma_start(dst, src).then_inc(ada_loaded[slot], 16)

            for m in range(M):
                sp.dma_start(x_sb[:, m], x_dram[:, m]).then_inc(x_loaded[m], 16)

            def ada_slot_free(a):
                b = a - (RING_0 if a < ADA_0 + RING else RING)
                if b < 0:
                    return
                if b >= ADA_0:
                    sp.wait_ge(ada_on_dve, ADA_0_DVE + (b - ADA_0) + 1)
                elif b % PE_EVERY == 0:
                    sp.wait_ge(ada_on_pe, b // PE_EVERY + 1)
                else:
                    sp.wait_ge(ada_on_dve, b - b // PE_EVERY)

            def load_straight(t):
                job, kc, _, _ = STRAIGHT[t]
                if job < NJ:
                    src = chunked(w_in[0], kc, TK, IN_COLS[job], N)
                else:
                    src = chunked(w_out[0], kc, TK, (job - NJ) * N, N)
                load_weight(t, t % RING, src, first=t < RING)

            for q in range(QUARTERS):
                for kc in range(KC):
                    a = q * KC + kc
                    ada_slot_free(a)
                    load_ada(ada_slot(a), wada[kc * P:(kc + 1) * P, 0:2 * D].rearrange(
                        "p (g n) -> p g n", g=2)[:, :, q * (AC // 2):(q + 1) * (AC // 2)])
                    if q and kc in MIX_AT:
                        load_straight((q - 1) * len(MIX_AT) + MIX_AT.index(kc))
            for t in range(Q_TILES - len(MIX_AT), NS):
                load_straight(t)
                for u in ada_beside(t):
                    a = ADA_0 + u
                    ada_slot_free(a)
                    blk, k = 4 + u // KC, u % KC
                    load_ada(ada_slot(a), wada[k * P:(k + 1) * P, blk * AC:(blk + 1) * AC])
            def gate_up(i, t0, f0, gate2):
                for u in range(2 * JOB_TILES):
                    w = w_gate[0] if u < JOB_TILES else w_up[0]
                    load_weight(i * (2 * JOB_TILES) + (t0 + u), u % RING,
                                chunked(w, TK * (u % JOB_TILES), TK, i * N + f0 * N, N))
                    if gate2 == 1:
                        for n in gate2_peeled(u - LEAD):
                            ada_slot_free(G2_0 + n)
                            load_ada(ada_slot(G2_0 + n), wada[n // 2 * P:(n // 2 + 1) * P,
                                                              (10 + n % 2) * AC:(11 + n % 2) * AC])
                    elif gate2 and u - LEAD in GATE2_LOOP:
                        v = GATE2_LOOP.index(u - LEAD)
                        sp.wait_ge(ada_on_dve, i * 4 + (G2_LOOP + v - RING + 1))
                        load_ada(v, wada[bass.ds(i * (2 * P) + (KC // 2 - 2 + v // 2) * P, P),
                                         (10 + v % 2) * AC:(11 + v % 2) * AC])

            gate_up(0, T_GA, 0, 1)
            with sp.Fori(1, FA - 1) as i:
                gate_up(i, T_GA, 0, 0.25)
            gate_up(FA - 1, T_GA, 0, 0)

            def down(t0, f0, tiles, steps):
                with sp.Fori(0, steps) as i:
                    for u in range(2 * tiles):
                        jj, v = divmod(u, tiles)
                        load_weight(i * (2 * tiles) + (t0 + u), u % RING,
                                    chunked(w_down[0], f0 + TK * v, TK, i * (2 * N) + jj * N, N))

            down(T_DA, 0, DT_A, OUT_JOBS // 2)
            sp.wait_ge(block_reduced, 12)
            sp.dma_start(final_row, final_norm_w.partition_broadcast(P)).then_inc(final_loaded, 16)
            with sp.Fori(0, FB) as i:
                gate_up(i, T_GB, FA, 0)
            down(T_DB, 4 * FA, DT_B, OUT_JOBS // 2)
            for half in range(2):
                sp.wait_ge(y_ready[0], half + 1)
                sp.dma_start(out_dram[:, 0, half * AC:(half + 1) * AC],
                             y_sb[:, 0, half * AC:(half + 1) * AC]).then_inc(out_stored, 16)
            sp.wait_ge(out_stored, 64)

        @block.tensor
        def _(pe):
            def transpose(dst, src, n=P):
                return pe.transpose(dst, src, ident[0:n, 0:n])

            def products(t, slot, pair, lhs, first, last):
                pe.wait_ge(lo_ready, t + 1)
                for kk in range(TK):
                    for m in range(M):
                        hi, lo = lhs(kk, m)
                        dst = misc_ps[:, 1 + m] if pair == 2 else acc_ps[:, 2 * pair + m]
                        pe.matmul(dst, hi, w_hi[:, slot, kk], start=first and kk == 0, stop=False)
                        pe.matmul(dst, hi, w_lo[:, slot, kk], start=False, stop=False)
                        mm = pe.matmul(dst, lo, w_hi[:, slot, kk], start=False,
                                       stop=last and kk == TK - 1)
                mm.then_inc(tile_done, 1)

            def of_h(kc):
                return lambda kk, m: (h_hi[:, kc + kk, m * P:(m + 1) * P],
                                      h_lo[:, kc + kk, m * P:(m + 1) * P])

            def of_mixed(kc):
                if kc >= HH:
                    return lambda kk, m: (mixa_hi[:, kc - HH + kk, m * P:(m + 1) * P],
                                          mixa_lo[:, kc - HH + kk, m * P:(m + 1) * P])
                return of_h(kc)

            def of_hidden(kc):
                return lambda kk, m: (hid_hi[:, kc + kk, m * P:(m + 1) * P],
                                      hid_lo[:, kc + kk, m * P:(m + 1) * P])

            def reduce_block(q, buf, col):
                pe.wait_ge(block_summed, q + 1)
                for cc in range(8):
                    mm = pe.matmul(small_ps[:, bass.ds(col + cc, 1)], acc[:, buf, cc * P:(cc + 1) * P],
                                   ones[:], start=False, stop=False, skip_group_check=True)
                mm.then_inc(block_reduced, 1)

            def turn_x(norm, kp, banks):
                pe.wait_ge(xn_ready, 2 if norm == 0 else 2 + 2 * (kp // 2 + 1))
                if kp >= banks:
                    pe.wait_ge(modulated_ready, 8 * norm + kp - banks + 1)
                for j in range(2):
                    for m in range(M):
                        kc = 2 * kp + j
                        tr = transpose(misc_ps[:, kp % banks, j * S + m * P:j * S + (m + 1) * P],
                                       xn[:, m, kc * P:(kc + 1) * P])
                tr.then_inc(xn_turned, 1)

            pe.wait_ge(consts_ready, 1)
            pe.wait_ge(vec_loaded, 16 * 5)
            transpose(misc_ps[:, 2, 0:3 * KC + HH], vec_rows[:], 3 * KC + HH)
            transpose(misc_ps[:, 2, P:P + 6 * KC], bada_rows[:], 6 * KC).then_inc(vec_turned, 1)
            pe.wait_ge(c_ready, 1)
            pe.matmul(small_ps[:, N - 1:N], ident[:], ones[:], start=True, stop=False,
                      skip_group_check=True)

            def ada_tile(q, kc):
                a = q * KC + kc
                pe.wait_ge(ada_loaded[ada_slot(a)], ada_turn(a))
                for cc in range(8):
                    mm = pe.matmul(small_ps[:, 8 * q + cc:8 * q + cc + 1],
                                   ada_at(ada_slot(a))[:, cc * P:(cc + 1) * P], c_act[:, kc:kc + 1],
                                   start=False, stop=False, skip_group_check=True)
                mm.then_inc(ada_on_pe, 1)

            def att_scores(p):
                pe.wait_ge(qk_ready, 3)
                if p:
                    pe.wait_ge(probsT_ready, p)
                for a in range(2):
                    r = slice(DH * a, DH * a + DH)
                    h = 2 * p + a
                    pe.wait_ge(bias_loaded[h % 4], 16 * (h // 4 + 1))
                    for q, dst in ((0, misc_ps[:, a, 0:P]), (1, misc_ps[:, a, P:3 * P])):
                        pe.matmul(dst, flip[:], bias[:, h % 4, (1 - q) * P:], start=True, stop=False)
                        mm = pe.matmul(dst, qT[r, p, q * P:(q + 1) * P], kT[r, p // 2, 0:(q + 1) * P],
                                       start=False, stop=True)
                mm.then_inc(scores_ready, 1)

            def att_turn(p):
                pe.wait_ge(exp_ready, p + 1)
                for a in range(2):
                    for j in range(3):
                        tr = transpose(misc_ps[:, a, j * P:(j + 1) * P], probs[:, a, j * P:(j + 1) * P])
                tr.then_inc(probs_turned, 1)

            def att_pv(p):
                pe.wait_ge(probsT_ready, p + 1)
                if p:
                    pe.wait_ge(mixa_lo_ready, p)
                else:
                    pe.wait_ge(c_ready, 1)
                v = slice(DH * (p // 2), DH * (p // 2) + DH)
                for a in range(2):
                    o0 = misc_ps[:, 2, a * DH:(a + 1) * DH]
                    o1 = misc_ps[:, 2, P + a * DH:P + (a + 1) * DH]
                    pe.matmul(o0, probsT[:, a, 0:P], v_att[:, 0, v], start=True, stop=True)
                    pe.matmul(o1, probsT[:, a, P:2 * P], v_att[:, 0, v], start=True, stop=False)
                    mm = pe.matmul(o1, probsT[:, a, 2 * P:3 * P], v_att[:, 1, v], start=False, stop=True)
                mm.then_inc(pv_ready, 1)

            def att_turn_out(p):
                pe.wait_ge(o_att_ready, p + 1)
                for m in range(M):
                    tr = transpose(misc_ps[:, 2, 2 * P + m * P:2 * P + (m + 1) * P], o_att[:, m])
                tr.then_inc(o_att_turned, 1)

            def hg_prepare(h):
                hc = slice(h * P, (h + 1) * P)
                if h == 0:
                    pe.wait_ge(logf_ready, 2)
                    pe.wait_ge(mod_ready, 6)
                    pe.wait_ge(probsT_ready, PAIRS)
                    pe.wait_ge(pair_free[pair_of(7)], job_free_count(7) + 2)
                else:
                    pe.wait_ge(hg_exp_ready, h)
                    pe.wait_ge(hg_ops_ready, h)
                    pe.wait_ge(hg_state_ready, h)
                if h == HH // 2:
                    pe.wait_ge(pair_free[pair_of(8)], job_free_count(8) + 2)
                for q in SUMS_BEFORE:
                    if h == SUMS_BEFORE[q]:
                        pe.wait_ge(mod_ready, q + 1)
                for m in range(M):
                    pe.matmul(misc_ps[:, 0, m * S:(m + 1) * S], g_tok[:, m, hc],
                              upper[:].rearrange("p a b -> p (a b)"), start=True, stop=True)
                for m in range(M):
                    transpose(misc_ps[:, 1, m * P:(m + 1) * P], q_tok[:, m, hc])
                    transpose(misc_ps[:, 1, S + m * P:S + (m + 1) * P], k_tok[:, m, hc])
                for m in range(M):
                    mm = pe.matmul(small_ps[:, m * P:(m + 1) * P], after[:], g_tok[:, m, hc],
                                   start=True, stop=True, skip_group_check=True)
                mm.then_inc(sums_ready, 1)

            def hg_core(h):
                hc = slice(h * P, (h + 1) * P)
                t = hg[:, h % 2]
                pe.wait_ge(hg_ops_ready, h + 1)
                if h:
                    pe.wait_ge(hg_out_taken, h)
                else:
                    pe.wait_ge(mixa_lo_ready, PAIRS)
                for m in range(M):
                    pe.matmul(misc_ps[:, 2, m * P:(m + 1) * P], t[:, 1, m * P:(m + 1) * P],
                              t[:, 0, m * P:(m + 1) * P], start=True, stop=True)
                for ch in range(3):
                    m, r = ch // 2, slice(CH * (ch % 2), CH * (ch % 2) + CH)
                    dst = (misc_ps[:, 2, S:S + P], misc_ps[:, 0, 0:P], misc_ps[:, 2, S + P:S + 2 * P])[ch]
                    mm = pe.matmul(dst, t[r, 3, m * P:(m + 1) * P], v_tok[r, m, hc],
                                   start=True, stop=True)
                mm.then_inc(hg_scores_ready, 1)

            def hg_out(h):
                hc = slice(h * P, (h + 1) * P)
                t = hg[:, h % 2]
                pe.wait_ge(hg_state_ready, h + 1)
                for m in range(M):
                    cs = slice(m * P, (m + 1) * P)
                    pe.matmul(misc_ps[:, 2, cs], att[:, m], v_tok[:, m, hc],
                              start=True, stop=False, skip_group_check=True)
                    for r in range(2):
                        ch = 2 * m + r
                        if ch:
                            mm = pe.matmul(misc_ps[CH * r:CH * r + CH, 2, cs],
                                           t[:, 2, ch * CH:(ch + 1) * CH], state[:, ch - 1],
                                           start=False, stop=True, skip_group_check=True)
                mm.then_inc(hg_out_ready, 1)

            def hg_turn(i):
                pe.wait_ge(hg_normed, i + 1)
                if i == 0:
                    pe.wait_ge(hg_out_taken, HH)
                if i == 3:
                    pe.wait_ge(mixr_tmp_ready, 1)
                for j in range(2):
                    for m in range(M):
                        h = 2 * i + j
                        tr = transpose(misc_ps[:, i % 3, j * S + m * P:j * S + (m + 1) * P],
                                       k_tok[:, m, h * P:(h + 1) * P])
                tr.then_inc(hg_turned, 1)

            def spread_gate(n, col, which):
                if n == 3:
                    pe.wait_ge(gate_row_ready, 4 * which + 1)
                for j in range(4):
                    mm = pe.matmul(misc_ps[:, n % 3, j * P:(j + 1) * P],
                                   mod[:, col + 4 * n + j:col + 4 * n + j + 1].to_broadcast([P, P]),
                                   ident[:], start=True, stop=True)
                mm.then_inc(gate_spread, 1)

            def gap(g):
                if g in Q_GAPS:
                    u = Q_GAPS.index(g)
                    pe.wait_ge(pair_free[u], 2)
                    if u == 0:
                        pe.wait_ge(pair_free[2], 2)
                    else:
                        pe.wait_ge(qk_ready, u)
                    for b in range(4):
                        for m in range(M):
                            tr = transpose(misc_ps[:, b // 2, (b % 2) * S + m * P:(b % 2) * S + (m + 1) * P],
                                           k_tok[:, m, N * u + b * P:N * u + (b + 1) * P])
                    tr.then_inc(qk_turned, 1)
                if g == K_GAP:
                    pe.wait_ge(pair_free[2], 2)
                    pe.wait_ge(qk_ready, 2)
                    for b in range(4):
                        for m in range(M):
                            tr = transpose(misc_ps[:, b // 2, (b % 2) * S + m * P:(b % 2) * S + (m + 1) * P],
                                           k_dup[:, m, b].rearrange("p a b -> p (a b)"))
                    tr.then_inc(qk_turned, 1)
                if g in RED_GAP:
                    q = RED_GAP[g]
                    pe.wait_ge(mod_ready, q)
                    if q >= 6:
                        pe.wait_ge(hg_exp_ready, SUMS_BEFORE.get(q, HH))
                    reduce_block(q, q % 2, 8 * q)
                p, s = divmod(g - ATT_GAP, ATT_PERIOD)
                if s == 0 and 0 <= p - 1 < PAIRS:
                    att_turn_out(p - 1)
                if 0 <= p < PAIRS:
                    if s == 0:
                        att_scores(p)
                    if s == 2:
                        att_turn(p)
                    if s == 3:
                        att_pv(p)
                h, s = divmod(g - HG_GAP, HG_PERIOD)
                if s == 0:
                    if 0 <= h - 1 < HH:
                        hg_out(h - 1)
                    if 0 <= h < HH:
                        hg_prepare(h)
                if s == 2 and 0 <= h < HH:
                    hg_core(h)
                for i in range(4):
                    if FIN_GAPS[i] == g:
                        hg_turn(i)
                    if G1_GAPS[i] == g:
                        if i == 0:
                            pe.wait_ge(mixr_tmp_ready, 4)
                        spread_gate(i, GATE1, 0)

            def straight(t):
                job, kc, first, last = STRAIGHT[t]
                if first and job >= QJ:
                    pe.wait_ge(pair_free[pair_of(job)], job_free_count(job))
                if job == 0:
                    pe.wait_ge(h_lo_ready, kc // 2 + 1)
                if job >= NJ:
                    if kc >= HH:
                        pe.wait_ge(mixa_lo_ready, PAIRS)
                    else:
                        pe.wait_ge(mixr_lo_ready, kc // 2 + 1)
                products(t, t % RING, pair_of(job), of_h(kc) if job < NJ else of_mixed(kc), first, last)
                gap(t)

            for kc in range(0, KC, PE_EVERY):
                ada_tile(0, kc)
            for q in range(QUARTERS):
                reduce_block(q, q % 2, 8 * q)
                turn_x(0, 2 * q, 1)
                pe.wait_ge(mod_ready, q + 1)
                if q + 1 < QUARTERS:
                    ada_tile(q + 1, 0)
                turn_x(0, 2 * q + 1, 1)
                if q + 1 < QUARTERS:
                    for kc in range(1, KC):
                        if kc % PE_EVERY == 0:
                            ada_tile(q + 1, kc)
                        if kc in MIX_AT:
                            straight(q * len(MIX_AT) + MIX_AT.index(kc))
            for t in range(Q_TILES - len(MIX_AT), NS):
                straight(t)

            for kp in range(2):
                turn_x(1, kp, 2)

            def turn_hidden(count):
                pe.wait_ge(hid_t_ready, count * 2 + 2)
                pe.wait_ge(hid_lo_ready, count * 2)
                for b in range(2):
                    for j in range(2):
                        for m in range(M):
                            tr = transpose(misc_ps[:, b, j * S + m * P:j * S + (m + 1) * P],
                                           hid_t[:, m, (2 * b + j) * P:(2 * b + j + 1) * P])
                    tr.then_inc(hid_turned, 1)

            def gate_up(i, t0, job0, before, peeled, gate2_gaps=False):
                for jj in range(2):
                    job = job0 + jj
                    pe.wait_ge(pair_free[pair_of(job)], i * 2 + job_free_count(job))
                    for v in range(JOB_TILES):
                        u = jj * JOB_TILES + v
                        if peeled and before == 0 and jj == 0:
                            if v + 2 < KC // 2:
                                turn_x(1, v + 2, 2)
                            pe.wait_ge(h_lo_ready, 8 + v + 1)
                        products(i * (2 * JOB_TILES) + (t0 + u), u % RING, pair_of(job), of_h(TK * v),
                                 v == 0, v == JOB_TILES - 1)
                        if gate2_gaps and u in (4, 6):
                            q = 8 + u // 2
                            reduce_block(q, q % 2, 8 * q)
                        if gate2_gaps and u == 8:
                            pe.wait_ge(mod_ready, 11)
                            pe.wait_ge(hid_lo_ready, 2 * i)
                            for n in range(4):
                                spread_gate(n, GATE2, 1)
                        if not peeled and u == 2:
                            turn_hidden(i + (before - 1))

            def down(t0, job0, tiles, steps, count):
                def two_jobs(i, peeled):
                    for jj in range(2):
                        job = job0 + jj
                        pe.wait_ge(pair_free[pair_of(job)], i * 2 + job_free_count(job))
                        for v in range(tiles):
                            if peeled and jj == 0 and v == 2:
                                if count == FA - 1:
                                    pe.wait_ge(gate_row_ready, 8)
                                turn_hidden(count)
                            if v == tiles - 2:
                                pe.wait_ge(hid_lo_ready, 2 * count + 2)
                            u = jj * tiles + v
                            products(i * (2 * tiles) + (t0 + u), u % RING, pair_of(job),
                                     of_hidden(TK * v), v == 0, v == tiles - 1)

                two_jobs(0, True)
                with pe.Fori(1, steps) as i:
                    two_jobs(i, False)

            gate_up(0, T_GA, JOB_GA, 0, True)
            with pe.Fori(1, FA - 1) as i:
                gate_up(i, T_GA, JOB_GA, 0, False)
            gate_up(FA - 1, T_GA, JOB_GA, 0, False, gate2_gaps=True)
            down(T_DA, JOB_DA, DT_A, OUT_JOBS // 2, FA - 1)
            gate_up(0, T_GB, JOB_GB, FA, True)
            with pe.Fori(1, FB) as i:
                gate_up(i, T_GB, JOB_GB, FA, False)
            down(T_DB, JOB_DB, DT_B, OUT_JOBS // 2, FJ - 1)

        @block.scalar
        def _(act):
            chain = [0]

            def link(ins):
                chain[0] += 1
                ins.then_inc(act_chain, 1)
                act.wait_ge(act_chain, chain[0])

            def split(t, slot, turn, first=False):
                act.wait_ge(weight_loaded[slot], turn)
                if not first:
                    act.wait_ge(tile_done, t - (RING - 1))
                act.copy(w_hi[:, slot], w_raw[:, slot]).then_inc(hi_ready, 1)

            def split_s(t):
                if t < T_END:
                    split(t, t % RING, 16 * (t // RING + 1), first=t < RING)

            def split_r(i, per, t0, u):
                split(i * per + (t0 + u), u % RING, i * (16 * per // RING) + 16 * ((t0 + u) // RING + 1))

            def h_heads(norm, kp, banks):
                shift = SHIFT1 if norm == 0 else SHIFT2
                act.wait_ge(gain_ready, kp // 2 + 1 if norm == 0 else QUARTERS + 1)
                act.wait_ge(xn_turned, 8 * norm + kp + 1)
                if kp >= 2:
                    act.wait_ge(h_lo_ready, 8 * norm + kp - 1)
                for j in range(2):
                    kc = 2 * kp + j
                    ins = act.activation(modulated[:, kp % 2, j], misc_ps[:, kp % banks, j * S:(j + 1) * S],
                                         ACT.Identity, bias=mod[:, shift + kc:shift + kc + 1],
                                         scale=gain[:, kc:kc + 1])
                ins.then_inc(modulated_ready, 1)
                act.wait_ge(modulated_ready, 8 * norm + kp + 1)
                act.copy(h_hi[:, 2 * kp:2 * kp + 2, :], modulated[:, kp % 2]).then_inc(h_hi_ready, 1)

            for dst, src in ((vec_rows[0:KC], c.rearrange("b (r q) -> (b r) q", q=P)),
                             (vec_rows[KC:2 * KC], norm1_w.rearrange("b (r q) -> (b r) q", q=P)),
                             (vec_rows[2 * KC:3 * KC], norm2_w.rearrange("b (r q) -> (b r) q", q=P)),
                             (vec_rows[3 * KC:3 * KC + HH], hgrn_norm_w.rearrange("b (r q) -> (b r) q", q=P)),
                             (bada_rows[:], b_ada.rearrange("b (r q) -> (b r) q", q=P))):
                act.dma_start(dst, src).then_inc(vec_loaded, 16)
            act.dma_start(sink[:], attn_sinks[0].partition_broadcast(P)).then_inc(sink_loaded, 16)

            act.wait_ge(vec_turned, 1)
            act.activation(c_act[:], misc_ps[:, 2, 0:KC], ACT.Silu)
            act.copy(cols[:], misc_ps[:, 2, KC:3 * KC + HH])
            act.copy(bada[:], misc_ps[:, 2, P:P + 6 * KC]).then_inc(c_ready, 1)
            for m in range(M):
                act.wait_ge(x_loaded[m], 16)
                ins = act.activation(xn[:, m], x_sb[:, m], ACT.Square, accum_out=stat[:, m:m + 1])
                ins.then_inc(squares_ready, 1)
            act.wait_ge(root_ready, 1)
            act.wait_ge(squares_ready, 2)
            for m in range(M):
                act.activation(xn[:, m], x_sb[:, m], ACT.Copy, scale=stat[:, 12 + m:13 + m]).then_inc(xn_ready, 1)
            for q in range(QUARTERS):
                for kp in (2 * q, 2 * q + 1):
                    h_heads(0, kp, 1)
                for t in range(q * len(MIX_AT), (q + 1) * len(MIX_AT)):
                    split_s(t)

            act.dma_start(low[:], lower_bounds.partition_broadcast(P)).then_inc(low_loaded, 16)

            def take_in(job):
                act.wait_ge(tile_done, JOB_END[job] + 1)
                kind, half = divmod(job - 3, 2)
                cs = slice(N * half, N * half + N)
                if job == 3:
                    act.wait_ge(qk_turned, 3)
                    act.wait_ge(low_step, 6)
                if job == 7:
                    act.wait_ge(f_ready, 4)
                if job == 9:
                    act.wait_ge(scores_ready, PAIRS)
                for m in range(M):
                    src = bank_of(job, m)
                    if job < 2:
                        ins = act.copy(k_tok[:, m, N * job:N * job + N], src)
                    elif job == 2:
                        s4 = src[:, 0:4 * DH].rearrange("p (g d) -> p g d", g=4)
                        act.copy(k_dup[:, m, :, 0, :], s4)
                        act.copy(k_dup[:, m, :, 1, :], s4)
                        ins = act.copy(v_att[:, m], src[:, 4 * DH:8 * DH])
                    elif kind == 0:
                        ins = act.activation(g_tok[:, m, cs], src, ACT.Sigmoid)
                    elif kind == 1:
                        ins = act.copy(v_tok[:, m, cs], src)
                    elif kind == 2:
                        ins = act.copy(q_tok[:, m, cs], src)
                    else:
                        ins = act.activation(silu_g[:, m, cs], src, ACT.Silu)
                    ins.then_inc(pair_free[pair_of(job)], 1)

            def att_exp(p):
                act.wait_ge(max_ready, p + 1)
                for a in range(2):
                    act.activation(probs[:, a, 0:P], misc_ps[:, a, 0:P], ACT.Exp,
                                   bias=stat[:, 20 + 2 * a:21 + 2 * a], accum_out=stat[:, 28 + 2 * a:29 + 2 * a])
                    act.activation(probs[:, a, P:3 * P], misc_ps[:, a, P:3 * P], ACT.Exp,
                                   bias=stat[:, 21 + 2 * a:22 + 2 * a], accum_out=stat[:, 29 + 2 * a:30 + 2 * a])
                act.activation(stat[:, 24:28], stat[:, 24:28], ACT.Exp).then_inc(exp_ready, 1)

            def hg_exp(h):
                act.wait_ge(sums_ready, h + 1)
                if h >= 2:
                    act.wait_ge(hg_out_ready, h - 1)
                t = hg[:, h % 2]
                rel = misc_ps[:, 0].rearrange("p (m a t) -> p m a t", m=M, a=2)
                two = lambda i: t[:, i].rearrange("p (m t) -> p m t", m=M)
                act.activation(two(0), rel[:, :, 0], ACT.Exp)
                act.activation(two(1), rel[:, :, 0], ACT.Exp, scale=-1.0)
                act.activation(two(2), rel[:, :, 1], ACT.Exp)
                act.activation(t[:, 3], small_ps[:, 0:S], ACT.Exp).then_inc(hg_exp_ready, 1)

            def hg_take(h):
                act.wait_ge(hg_out_ready, h + 1)
                src = misc_ps[:, 2, 0:S].rearrange("p (m t) -> p m t", m=M)
                act.copy(k_tok[:, :, h * P:(h + 1) * P], src)
                if h:
                    act.wait_ge(hg_out_taken, h)
                for m in range(M):
                    ins = act.activation(junk[:, m], misc_ps[:, 2, m * P:(m + 1) * P], ACT.Square,
                                         accum_out=stat[:, 32 + m * HH + h:33 + m * HH + h])
                ins.then_inc(hg_out_taken, 1)

            def gate_row_take(n, dst, which):
                act.wait_ge(gate_spread, 4 * which + n + 1)
                act.copy(dst[:, n * N:(n + 1) * N], misc_ps[:, n % 3]).then_inc(gate_row_ready, 1)

            def squares_of(n, count, before):
                act.wait_ge(squares_ready, before)
                for m in range(M):
                    act.wait_ge(x_updated, count + m - 1)
                    ins = act.activation(sq_junk[:, m], x_sb[:, m, n * N:(n + 1) * N], ACT.Square,
                                         accum_out=stat[:, m * 4 + n:m * 4 + n + 1])
                ins.then_inc(squares_ready, 1)

            def gap(g):
                if g in Q_GAPS or g == K_GAP:
                    u = (*Q_GAPS, K_GAP).index(g)
                    act.wait_ge(qk_turned, u + 1)
                    act.wait_ge(bias_stored, 16)
                    for b in range(2):
                        src = misc_ps[:, b].rearrange("p (a t) -> p a t", a=2)
                        if u < 2:
                            ins = act.mul(qT[:, 4 * u + 2 * b:4 * u + 2 * b + 2], src, DH ** -0.5)
                        else:
                            ins = act.copy(kT[:, 2 * b:2 * b + 2], src)
                    ins.then_inc(qk_ready, 1)
                if g == LOW_GAPS[1]:
                    act.wait_ge(low_step, 2)
                    act.activation(low[:], low[:], ACT.Exp).then_inc(low_step, 1)
                for job, end in JOB_END.items():
                    if max(end, Q_TILES - LEAD) == g and job < NJ:
                        take_in(job)
                if g == JOB_END[4] + 3:
                    act.wait_ge(f_ready, 4)
                    for m in range(M):
                        act.activation(g_tok[:, m], g_tok[:, m], ACT.Ln).then_inc(logf_ready, 1)
                p, s = divmod(g - ATT_GAP, ATT_PERIOD)
                if s == 0 and 0 <= p - 1 < PAIRS:
                    act.wait_ge(o_att_turned, p)
                    act.copy(mixa_hi[:, p - 1], misc_ps[:, 2, 2 * P:4 * P]).then_inc(mixa_hi_ready, 1)
                if 0 <= p < PAIRS:
                    if s == 0:
                        att_exp(p)
                    if s == 2:
                        act.wait_ge(probs_turned, p + 1)
                        for a in range(2):
                            ins = act.copy(probsT[:, a], misc_ps[:, a, 0:3 * P])
                        ins.then_inc(probsT_ready, 1)
                h, s = divmod(g - HG_GAP, HG_PERIOD)
                if s == 0:
                    if 0 <= h - 1 < HH:
                        hg_take(h - 1)
                    if 0 <= h < HH:
                        hg_exp(h)
                for i in range(4):
                    if FIN_GAPS[i] == g:
                        act.wait_ge(hg_turned, i + 1)
                        if i >= 2:
                            act.wait_ge(mixr_lo_ready, i - 1)
                        for j in range(2):
                            h = 2 * i + j
                            ins = act.activation(modulated[:, i % 2, j], misc_ps[:, i % 3, j * S:(j + 1) * S],
                                                 ACT.Copy, scale=cols[:, 2 * KC + h:2 * KC + h + 1])
                        ins.then_inc(mixr_tmp_ready, 1)
                        act.wait_ge(mixr_tmp_ready, i + 1)
                        act.copy(h_hi[:, 2 * i:2 * i + 2], modulated[:, i % 2]).then_inc(mixr_hi_ready, 1)
                    if G1_GAPS[i] == g:
                        gate_row_take(i, gate1_row, 0)
                for job, end in JOB_END.items():
                    if min(end + 1, NS - 1) == g and job >= NJ:
                        squares_of(job - NJ, 2 * (job - NJ) + 2, 2 + job - NJ)

            for t in range(Q_TILES - LEAD, NS):
                split_s(t + LEAD)
                gap(t)
            for kp in range(LEAD):
                h_heads(1, kp, 2)

            def hidden_head(it, dst0):
                for b in range(2):
                    act.wait_ge(hid_turned, it * 2 + (b + 1))
                    act.copy(hid_hi[:, bass.ds(dst0 + 2 * b, 2), :],
                             misc_ps[:, b].rearrange("p (a t) -> p a t", a=2)).then_inc(hid_hi_ready, 1)

            def gate_up(i, t0, job0, before, peeled, gate2_gaps=False):
                for u in range(2 * JOB_TILES):
                    split_r(i, 2 * JOB_TILES, t0, u + LEAD)
                    if peeled and before == 0 and u + LEAD < KC // 2:
                        h_heads(1, u + LEAD, 2)
                    if u == 2 and not peeled:
                        hidden_head(i + (before - 1), i * 4 - 4)
                    if u == 8 and gate2_gaps:
                        for n in range(4):
                            gate_row_take(n, gate_row, 1)
                    if u == JOB_TILES - 1:
                        act.wait_ge(tile_done, i * (2 * JOB_TILES) + (t0 + JOB_TILES))
                        if not (peeled and before == 0):
                            act.wait_ge(hid_t_ready, i * 2 + 2 * before)
                        for m in range(M):
                            act.activation(hid_g[:, m], acc_ps[:, 2 * pair_of(job0) + m],
                                           ACT.Silu).then_inc(hid_g_ready, 1)
                        act.wait_ge(hid_g_ready, i * 2 + (2 * before + 2))
                        act.sem_inc(pair_free[pair_of(job0)], 2)

            gate_up(0, T_GA, JOB_GA, 0, True)
            with act.Fori(1, FA - 1) as i:
                gate_up(i, T_GA, JOB_GA, 0, False)
            gate_up(FA - 1, T_GA, JOB_GA, 0, False, gate2_gaps=True)
            hidden_head(FA - 1, 4 * FA - 4)
            with act.Fori(0, OUT_JOBS // 2) as i:
                for u in range(2 * DT_A):
                    split_r(i, 2 * DT_A, T_DA, u + LEAD)
            gate_up(0, T_GB, JOB_GB, FA, True)
            with act.Fori(1, FB) as i:
                gate_up(i, T_GB, JOB_GB, FA, False)
            hidden_head(FJ - 1, 4 * FB - 4)
            for t in range(T_DB, T_END):
                split_s(t + LEAD)
                n, v = divmod(t - T_DB, DT_B)
                if (n and v == 0) or t == T_END - 1:
                    n = n - 1 if v == 0 else n
                    squares_of(n, 2 * (2 * OUT_JOBS + n) + 2, 6 + n)
            act.wait_ge(weighted_ready, 4 * M)
            act.wait_ge(root_ready, 4)
            for half in range(2):
                hs = slice(half * AC, (half + 1) * AC)
                act.mul(y_sb[:, 1, hs], y_sb[:, 1, hs], stat[:, 13:14]).then_inc(y_ready[1], 1)
                act.wait_ge(y_ready[1], half + 1)
                act.dma_start(out_dram[:, 1, hs], y_sb[:, 1, hs]).then_inc(out_stored, 16)

        @block.vector
        def _(dve):
            chain = [0]

            def link(ins):
                chain[0] += 1
                ins.then_inc(dve_chain, 1)
                dve.wait_ge(dve_chain, chain[0])

            def split(t, slot):
                dve.wait_ge(hi_ready, t + 1)
                dve.tensor_tensor(w_lo[:, slot], w_raw[:, slot], w_hi[:, slot].bitcast(F32),
                                  ALU.subtract).then_inc(lo_ready, 1)

            def split_s(t):
                if t < T_END:
                    split(t, t % RING)

            def add_ada(slot, turn, count, buf, ccol, first):
                dve.wait_ge(ada_loaded[slot], turn)
                if first:
                    ins = dve.tensor_scalar(acc[:, buf], ada_at(slot), ccol, None, ALU.mult)
                else:
                    dve.wait_ge(ada_on_dve, count)
                    ins = dve.scalar_tensor_tensor(acc[:, buf], ada_at(slot), ccol, acc[:, buf],
                                                   ALU.mult, ALU.add)
                ins.then_inc(ada_on_dve, 1)

            def mean_root(parts):
                if parts:
                    for m in range(M):
                        ins = dve.tensor_reduce(stat[:, 10 + m:11 + m], stat[:, 4 * m:4 * m + 4], AX.X, ALU.add)
                    link(ins)
                    src = stat[:, 10:12]
                else:
                    src = stat[:, 0:2]
                dve.tensor_scalar(stat[:, 8:10], src, 1.0 / D, EPS, ALU.mult, ALU.add).then_inc(mean_ready, 1)

            def normalise(cs):
                for m in range(M):
                    dve.tensor_scalar(xn[:, m, cs], x_sb[:, m, cs], stat[:, 12 + m:13 + m], None,
                                      ALU.mult).then_inc(xn_ready, 1)

            def gains(norm, k0, n):
                scale = SCALE1 if norm == 0 else SCALE2
                link(dve.tensor_scalar(gain[:, k0:k0 + n], mod[:, scale + k0:scale + k0 + n], 1.0, None, ALU.add))
                dve.tensor_tensor(gain[:, k0:k0 + n], gain[:, k0:k0 + n],
                                  cols[:, norm * KC + k0:norm * KC + k0 + n], ALU.mult).then_inc(gain_ready, 1)

            def h_tail(norm, kp):
                dve.wait_ge(h_hi_ready, 8 * norm + kp + 1)
                dve.tensor_tensor(h_lo[:, 2 * kp:2 * kp + 2], modulated[:, kp % 2],
                                  h_hi[:, 2 * kp:2 * kp + 2].bitcast(F32),
                                  ALU.subtract).then_inc(h_lo_ready, 1)

            dve.wait_ge(c_ready, 1)
            dve.wait_ge(squares_ready, 2)
            mean_root(False)

            def ada_tile(q, kc):
                a = q * KC + kc
                if kc == 1 and q >= 2:
                    dve.wait_ge(block_reduced, q - 1)
                add_ada(ada_slot(a), ada_turn(a), a - a // PE_EVERY - 1, q % 2, c_act[:, kc:kc + 1], kc == 1)
                if kc == KC - 1:
                    dve.wait_ge(ada_on_dve, a - a // PE_EVERY)
                    dve.sem_inc(block_summed, 1)

            def take_block(q):
                dve.wait_ge(block_reduced, q + 1)
                src = small_ps[:, 8 * q:8 * q + 8]
                if q < 4:
                    four = lambda v: v[:, 0:2 * KC].rearrange("p (g c) -> p g c", g=2)[:, :, 4 * q:4 * q + 4]
                    link(dve.tensor_tensor(four(mod), src.rearrange("p (g c) -> p g c", g=2), four(bada), ALU.add))
                    dve.sem_inc(mod_ready, 1)
                else:
                    dve.tensor_tensor(mod[:, 8 * q:8 * q + 8], src, bada[:, 8 * q:8 * q + 8],
                                      ALU.add).then_inc(mod_ready, 1)

            for kc in range(KC):
                if kc % PE_EVERY:
                    ada_tile(0, kc)
            for q in range(QUARTERS):
                take_block(q)
                gains(0, 4 * q, 4)
                if q + 1 == QUARTERS:
                    for kp in (2 * q, 2 * q + 1):
                        h_tail(0, kp)
                else:
                    for kc in range(KC):
                        if kc % PE_EVERY:
                            ada_tile(q + 1, kc)
                        if kc in (1, 2):
                            h_tail(0, 2 * q + kc - 1)
                        if kc in MIX_AT:
                            split_s(q * len(MIX_AT) + MIX_AT.index(kc))
            for t in range(Q_TILES - len(MIX_AT), Q_TILES):
                split_s(t)

            def ada_s(t):
                for u in ada_beside(t):
                    a = ADA_0 + u
                    q, kc = 4 + u // KC, u % KC
                    if kc == 0:
                        dve.wait_ge(block_reduced, q - 1)
                    add_ada(ada_slot(a), ada_turn(a), ADA_0_DVE + u, q % 2, c_act[:, kc:kc + 1], kc == 0)
                    if kc == KC - 1:
                        dve.wait_ge(ada_on_dve, ADA_0_DVE + u + 1)
                        dve.sem_inc(block_summed, 1)

            def att_max(p):
                dve.wait_ge(scores_ready, p + 1)
                top = stat[:, 16:20].rearrange("p (a m) -> p a m", a=2)
                dve.tensor_reduce(top[:, :, 0], misc_ps[:, 0:2, 0:P], AX.X, ALU.max)
                link(dve.tensor_reduce(top[:, :, 1], misc_ps[:, 0:2, P:3 * P], AX.X, ALU.max))
                sk = sink[:, 2 * p:2 * p + 2].unsqueeze(2).to_broadcast([P, 2, 2])
                link(dve.tensor_tensor(top, top, sk, ALU.max))
                dve.tensor_scalar(stat[:, 20:24], stat[:, 16:20], -1.0, None, ALU.mult)
                dve.tensor_tensor(stat[:, 24:28].rearrange("p (a m) -> p a m", a=2), sk, top,
                                  ALU.subtract).then_inc(max_ready, 1)

            def att_den(p):
                dve.wait_ge(exp_ready, p + 1)
                link(dve.tensor_tensor(stat[:, 28:32], stat[:, 28:32], stat[:, 24:28], ALU.add))
                link(dve.reciprocal(stat[:, 28:32], stat[:, 28:32]))

            def att_out(p):
                dve.wait_ge(pv_ready, p + 1)
                rden = stat[:, 28:32].rearrange("p (a m) -> p m a", a=2).unsqueeze(3).to_broadcast([P, M, 2, DH])
                dve.tensor_tensor(o_att[:].rearrange("p m (a d) -> p m a d", a=2),
                                  misc_ps[:, 2, 0:S].rearrange("p (m a d) -> p m a d", m=M, a=2),
                                  rden, ALU.mult).then_inc(o_att_ready, 1)

            def hg_ops(h):
                t = hg[:, h % 2]
                hc = slice(h * P, (h + 1) * P)
                dve.wait_ge(hg_exp_ready, h + 1)
                link(dve.tensor_copy(decay[:], t[:, 2].rearrange("p (c t) -> p c t", c=4)[:, :, CH - 1]))
                q, k = misc_ps[:, 1, 0:S], misc_ps[:, 1, S:2 * S]
                dve.tensor_tensor(t[:, 0], q, t[:, 0], ALU.mult)
                dve.tensor_tensor(t[:, 1], k, t[:, 1], ALU.mult)
                dve.tensor_tensor(t[:, 2], q, t[:, 2], ALU.mult)
                t3 = t[:, 3].rearrange("p (m t) -> p m t", m=M)
                dve.tensor_tensor(t3, k_tok[:, :, hc], t3, ALU.mult).then_inc(hg_ops_ready, 1)

            def hg_state(h):
                dve.wait_ge(hg_scores_ready, h + 1)
                for m in range(M):
                    dve.copy_predicated(att[:, m], upper[:, 1].bitcast(I32), misc_ps[:, 2, m * P:(m + 1) * P])
                link(dve.tensor_copy(state[:, 0], misc_ps[:, 2, S:S + P]))
                link(dve.scalar_tensor_tensor(state[:, 1], state[:, 0], decay[:, 1:2],
                                              misc_ps[:, 0, 0:P], ALU.mult, ALU.add))
                dve.scalar_tensor_tensor(state[:, 2], state[:, 1], decay[:, 2:3],
                                         misc_ps[:, 2, S + P:S + 2 * P],
                                         ALU.mult, ALU.add).then_inc(hg_state_ready, 1)

            def hg_norm():
                dve.wait_ge(hg_out_taken, HH)
                dve.tensor_scalar(stat[:, 32:48], stat[:, 32:48], 1.0 / P, EPS,
                                  ALU.mult, ALU.add).then_inc(mean_ready, 1)
                dve.wait_ge(root_ready, 2)
                dve.wait_ge(pair_free[pair_of(10)], job_free_count(10) + 2)
                dve.wait_ge(pair_free[pair_of(9)], job_free_count(9) + 2)
                for h in range(HH):
                    for m in range(M):
                        hc = slice(h * P, (h + 1) * P)
                        ins = dve.scalar_tensor_tensor(k_tok[:, m, hc], k_tok[:, m, hc],
                                                       stat[:, 48 + m * HH + h:49 + m * HH + h],
                                                       silu_g[:, m, hc], ALU.mult, ALU.mult)
                    if h % 2:
                        ins.then_inc(hg_normed, 1)

            def take_gated(job, n0, row, end, count, col):
                dve.wait_ge(tile_done, end)
                if not (isinstance(count, int) and count == 0):
                    dve.wait_ge(x_updated, count * 2)
                for m in range(M):
                    dve.tensor_tensor(gated[:, m], acc_ps[:, 2 * pair_of(job) + m], row[:, bass.ds(col, N)],
                                      ALU.mult).then_inc(pair_free[pair_of(job)], 1)
                    dve.wait_ge(pair_free[pair_of(job)], n0 + (m - 1))
                    xs = x_sb[:, m, bass.ds(col, N)]
                    dve.tensor_tensor(xs, xs, gated[:, m], ALU.add).then_inc(x_updated, 1)

            def gap(g):
                if g == LOW_GAPS[0]:
                    dve.wait_ge(low_loaded, 16)
                    dve.tensor_tensor(low_t[:], low[:, 0], low[:, 1], ALU.max).then_inc(low_step, 1)
                if g == LOW_GAPS[2]:
                    dve.wait_ge(low_step, 4)
                    dve.reciprocal(low_t[:], low_t[:]).then_inc(low_step, 1)
                if g in RED_GAP:
                    take_block(RED_GAP[g])
                p, s = divmod(g - ATT_GAP, ATT_PERIOD)
                if s == 0 and 0 <= p - 1 < PAIRS:
                    dve.wait_ge(mixa_hi_ready, p)
                    dve.tensor_tensor(mixa_lo[:, p - 1], misc_ps[:, 2, 2 * P:4 * P],
                                      mixa_hi[:, p - 1].bitcast(F32), ALU.subtract).then_inc(mixa_lo_ready, 1)
                if 0 <= p < PAIRS:
                    if s == 0:
                        if p == 0:
                            dve.wait_ge(sink_loaded, 16)
                        att_max(p)
                    if s == 2:
                        att_den(p)
                    if s == 3:
                        att_out(p)
                h, s = divmod(g - HG_GAP, HG_PERIOD)
                if 0 <= h < HH:
                    if s == 0:
                        hg_ops(h)
                    if s == 2:
                        hg_state(h)
                if g == HG_GAP + HG_PERIOD * HH:
                    hg_norm()
                for i in range(4):
                    if FIN_GAPS[i] == g:
                        dve.wait_ge(mixr_hi_ready, i + 1)
                        dve.tensor_tensor(h_lo[:, 2 * i:2 * i + 2], modulated[:, i % 2],
                                          h_hi[:, 2 * i:2 * i + 2].bitcast(F32),
                                          ALU.subtract).then_inc(mixr_lo_ready, 1)
                for job, end in JOB_END.items():
                    if end == g and job >= NJ:
                        dve.wait_ge(gate_row_ready, 4)
                        take_gated(job, job_free_count(job) + 2, gate1_row, end + 1, job - NJ, (job - NJ) * N)

            dve.wait_ge(consts_ready, 1)
            for t in range(Q_TILES - LEAD, NS):
                split_s(t + LEAD)
                gap(t)
                ada_s(t + LEAD)
            dve.wait_ge(modulated_ready, 8)
            gains(1, 0, KC)
            dve.wait_ge(squares_ready, 6)
            mean_root(True)
            dve.wait_ge(root_ready, 3)
            for i in range(4):
                normalise(slice(i * N, (i + 1) * N))
                if i:
                    h_tail(1, i - 1)
            h_tail(1, 3)

            def hidden_tail(it, dst0):
                for b in range(2):
                    dve.wait_ge(hid_hi_ready, it * 2 + (b + 1))
                    dst = bass.ds(dst0 + 2 * b, 2)
                    dve.tensor_tensor(hid_lo[:, dst, :], misc_ps[:, b].rearrange("p (a t) -> p a t", a=2),
                                      hid_hi[:, dst, :].bitcast(F32), ALU.subtract).then_inc(hid_lo_ready, 1)

            def gate_up(i, t0, job0, before, peeled, gate2):
                for u in range(2 * JOB_TILES):
                    split(i * (2 * JOB_TILES) + (t0 + u + LEAD), u % RING)
                    if peeled and before == 0 and u + LEAD < KC // 2:
                        h_tail(1, u + LEAD)
                    if gate2 == 1:
                        for n in gate2_peeled(u):
                            if n < 2:
                                dve.wait_ge(block_reduced, 9 + n)
                            add_ada(ada_slot(G2_0 + n), ada_turn(G2_0 + n), ADA_0_DVE + ADA_STRAIGHT + n,
                                    n % 2, c_act[:, n // 2:n // 2 + 1], n < 2)
                    elif gate2 and u in GATE2_LOOP:
                        v = GATE2_LOOP.index(u)
                        add_ada(v, i * 16 + (ada_turn(G2_0 + 2 * JOB_TILES) - 16), i * 4 + (G2_LOOP + v),
                                v % 2, c_act[:, bass.ds(i * 2 + (KC // 2 - 2 + v // 2), 1)], False)
                    if gate2 == 0 and before == 0 and u == 0:
                        dve.wait_ge(ada_on_dve, ADA_0_DVE + ADA_STRAIGHT + 2 * KC)
                        dve.sem_inc(block_summed, 2)
                    if gate2 == 0 and before == 0 and u == 7:
                        dve.wait_ge(block_reduced, 12)
                        dve.tensor_tensor(mod[:, GATE2:GATE2 + KC], small_ps[:, GATE2:GATE2 + KC],
                                          bada[:, GATE2:GATE2 + KC], ALU.add).then_inc(mod_ready, 1)
                    if u == 2 and not peeled:
                        hidden_tail(i + (before - 1), i * 4 - 4)
                    if u == 2 * JOB_TILES - 1:
                        dve.wait_ge(tile_done, i * (2 * JOB_TILES) + (t0 + 2 * JOB_TILES))
                        dve.wait_ge(hid_g_ready, i * 2 + (2 * before + 2))
                        if not (peeled and before == 0):
                            dve.wait_ge(hid_turned, i * 2 + 2 * before)
                        for m in range(M):
                            dve.tensor_tensor(hid_t[:, m], acc_ps[:, 2 * pair_of(job0 + 1) + m], hid_g[:, m],
                                              ALU.mult).then_inc(hid_t_ready, 1)
                        dve.wait_ge(hid_t_ready, i * 2 + (2 * before + 2))
                        dve.sem_inc(pair_free[pair_of(job0 + 1)], 2)

            def down(i, t0, job0, tiles, before):
                for u in range(2 * tiles):
                    if isinstance(i, int):
                        split_s(t0 + 2 * tiles * i + u + LEAD)
                    else:
                        split(i * (2 * tiles) + (t0 + u + LEAD), u % RING)
                    jj, v = divmod(u, tiles)
                    if v == tiles - 1:
                        job = job0 + jj
                        take_gated(job, i * 2 + (job_free_count(job) + 2), gate_row,
                                   i * (2 * tiles) + (t0 + (jj + 1) * tiles), i * 2 + (before + jj),
                                   i * (2 * N) + jj * N)
                        if before > OUT_JOBS:
                            cs = slice((2 * i + jj) * N, (2 * i + jj + 1) * N)
                            dve.wait_ge(x_updated, 2 * (2 * i + before + jj) + 2)
                            for m in range(M):
                                dve.tensor_tensor(y_sb[:, m, cs], x_sb[:, m, cs], final_row[:, cs],
                                                  ALU.mult).then_inc(weighted_ready, 1)

            gate_up(0, T_GA, JOB_GA, 0, True, 1)
            with dve.Fori(1, FA - 1) as i:
                gate_up(i, T_GA, JOB_GA, 0, False, 0.25)
            gate_up(FA - 1, T_GA, JOB_GA, 0, False, 0)
            hidden_tail(FA - 1, 4 * FA - 4)
            dve.wait_ge(gate_row_ready, 8)
            with dve.Fori(0, OUT_JOBS // 2) as i:
                down(i, T_DA, JOB_DA, DT_A, OUT_JOBS)
            gate_up(0, T_GB, JOB_GB, FA, True, 0)
            with dve.Fori(1, FB) as i:
                gate_up(i, T_GB, JOB_GB, FA, False, 0)
            hidden_tail(FJ - 1, 4 * FB - 4)
            dve.wait_ge(final_loaded, 16)
            for i in range(OUT_JOBS // 2):
                down(i, T_DB, JOB_DB, DT_B, 2 * OUT_JOBS)
            dve.wait_ge(squares_ready, 10)
            mean_root(True)
            dve.wait_ge(root_ready, 4)
            dve.wait_ge(weighted_ready, 4 * M)
            for half in range(2):
                hs = slice(half * AC, (half + 1) * AC)
                dve.tensor_scalar(y_sb[:, 0, hs], y_sb[:, 0, hs], stat[:, 12:13], None,
                                  ALU.mult).then_inc(y_ready[0], 1)

        @block.gpsimd
        def _(pool):
            chain = [0]

            def link(ins):
                chain[0] += 1
                ins.then_inc(pool_chain, 1)
                pool.wait_ge(pool_chain, chain[0])

            def keep(ap, pattern, base, mult, op=ALU.is_ge, fill=0.0):
                link(pool.affine_select(out=ap, in_=ap, compare_op=op, fill=fill, base=base,
                                        pattern=pattern, channel_multiplier=mult))

            up, rel = upper[:, 1], upper[:, 0]
            pool.memset(ones[:], 1.0)
            link(pool.memset(minus_half[:], -0.5))
            link(pool.memset(ident[:], 0.0))
            keep(ident[:], [[-1, P]], 0, 1, ALU.not_equal, 1.0)
            link(pool.memset(flip[:], 0.0))
            keep(flip[:], [[1, P]], 1 - P, 1, ALU.not_equal, 1.0)
            link(pool.memset(upper[:], 1.0))
            keep(up, [[1, P]], 0, -1)
            keep(up[:, CH:P], [[0, CH]], -CH, 1)
            keep(rel[:, 0:CH], [[0, CH]], CH // 2 - 1, -1)
            keep(rel[:, CH:P], [[0, CH]], -CH, 1)
            keep(rel[:, CH:P], [[0, CH]], CH + CH // 2 - 1, -1)
            link(pool.tensor_tensor(rel, up, rel, ALU.subtract))
            link(pool.memset(after[:], 1.0))
            keep(after[:], [[-1, P]], 0, 1, ALU.is_gt)
            keep(after[:, 0:CH], [[0, CH]], CH - 1, -1)
            link(pool.memset(att[:], 0.0))
            pool.sem_inc(consts_ready, 1)

            def inverse_root(count, dst, src):
                pool.wait_ge(mean_ready, count)
                pool.tensor_tensor(dst, src, minus_half[:, 0:src.shape[1]], ALU.pow).then_inc(root_ready, 1)

            pool.dma_start(table_t[:], rel_bias_table.rearrange("b h -> h b"),
                           allow_slow_non_contiguous=True).then_inc(table_loaded, 16)
            link(pool.memset(bias_row[:], NEG))
            inverse_root(1, stat[:, 12:14], stat[:, 8:10])
            pool.wait_ge(table_loaded, 16)
            for b, (lo, hi) in enumerate(bucket_ranges()):
                if lo > hi:
                    continue
                n = hi - lo + 1
                ins = pool.tensor_copy(bias_row[:, 2 * P - 1 - hi:2 * P - lo],
                                       table_t[:, b:b + 1].to_broadcast([AH, n]))
            link(ins)
            pool.dma_start(bias_dram, bias_row[:]).then_inc(bias_stored, 16)
            pool.wait_ge(bias_stored, 16)

            def load_bias(h):
                if h >= 4:
                    pool.wait_ge(scores_ready, (h - 4) // 2 + 1)
                pool.dma_start(bias[:, h % 4], bass.AP(bias_dram.tensor, h * 3 * P, [[1, P], [1, 2 * P]])
                               ).then_inc(bias_loaded[h % 4], 16)

            pool.wait_ge(low_step, 1)
            for j in range(2):
                ins = pool.tensor_tensor(low[:, j], low[:, j], low_t[:], ALU.subtract)
            ins.then_inc(low_step, 1)
            for h in range(4):
                load_bias(h)
            pool.wait_ge(low_step, 3)
            pool.tensor_tensor(low_t[:], low[:, 0], low[:, 1], ALU.add).then_inc(low_step, 1)
            pool.wait_ge(low_step, 5)
            for j in range(2):
                ins = pool.tensor_tensor(low[:, j], low[:, j], low_t[:], ALU.mult)
            ins.then_inc(low_step, 1)
            pool.wait_ge(low_step, 6)
            for half in range(2):
                cs = slice(half * N, half * N + N)
                if half == 0:
                    load_bias(4)
                    load_bias(5)
                job = 3 + half
                pool.wait_ge(pair_free[pair_of(job)], job_free_count(job) + 2)
                for m in range(M):
                    link(pool.tensor_tensor(k_tok[:, m, cs], g_tok[:, m, cs], low[:, 1, cs], ALU.mult))
                    link(pool.tensor_tensor(g_tok[:, m, cs], k_tok[:, m, cs], low[:, 0, cs], ALU.add))
                    pool.tensor_scalar(k_tok[:, m, cs], g_tok[:, m, cs], -1.0, 1.0, ALU.mult,
                                       ALU.add).then_inc(f_ready, 1)
            for h in range(6, AH):
                load_bias(h)
            inverse_root(2, stat[:, 48:64], stat[:, 32:48])
            inverse_root(3, stat[:, 12:14], stat[:, 8:10])
            inverse_root(4, stat[:, 12:14], stat[:, 8:10])


def bucket_ranges():
    import numpy as np
    half = REL_BUCKETS // 2
    d = np.arange(REL_MAX)
    log_b = half + (np.log(np.maximum(d, 1) / half) / np.log(REL_MAX / half)
                    * (REL_BUCKETS - half)).astype(np.int32)
    b = np.where(d < half, d, np.minimum(log_b, REL_BUCKETS - 1))
    out = []
    for i in range(REL_BUCKETS):
        w = np.nonzero(b == i)[0]
        out.append((int(w[0]), int(w[-1])) if len(w) else (1, 0))
    return out


_INS = ["x", "c", "w_ada", "b_ada", "norm1_w", "w_in", "lower_bounds", "hgrn_norm_w", "attn_sinks",
        "rel_bias_table", "w_out", "norm2_w", "w_gate", "w_up", "w_down", "final_norm_w"]


def kernel(**inputs):
    import numpy as _np
    import concourse.bacc as _bacc
    from concourse import mybir as _mybir
    from concourse.bass_utils import run_bass_kernel_spmd as _run

    nc = _bacc.Bacc("TRN2", target_bir_lowering=False, num_devices=1)
    arrays, args = {}, []
    for name in _INS:
        a = _np.ascontiguousarray(inputs[name])
        arrays[f"in_{name}"] = a
        args.append(nc.dram_tensor(f"in_{name}", a.shape, _mybir.dt.from_np(a.dtype), kind="ExternalInput").ap())
    args.append(nc.dram_tensor("out", (1, S, D), F32, kind="ExternalOutput").ap())
    build(nc, *args)
    r = _run(nc, [arrays], core_ids=[0])
    return r.results[0]["out"]
```
